# Optimizing a Trainium2 kernel written in Bass

```python
import math
import jax
import jax.numpy as jnp
from jax import lax
import numpy as np

D_MODEL = 1024
BATCH = 1
SEQ = 512
DEPTH = 2
DEC_BATCH = 8
DEC_SEQ = 8
PAST_LEN = 256
PAGE_SIZE = 128

SSD_HEADS = 6
SSD_HEAD_DIM = 64
SSD_INNER = SSD_HEADS * SSD_HEAD_DIM
SSD_GROUPS = 2
SSD_STATE = 128
SSD_CONV = 4
SSD_CONV_DIM = SSD_INNER + 2 * SSD_GROUPS * SSD_STATE
SSD_CHUNK = 64
GLA_HEADS = 4
GLA_HEAD_K = 32
GLA_HEAD_V = 64
GLA_DK = GLA_HEADS * GLA_HEAD_K
GLA_DV = GLA_HEADS * GLA_HEAD_V
GLA_GATE_RANK = 16
GLA_TAU = 16.0
GLA_CHUNK = 16
ATT_HEADS = 6
ATT_HEAD_DIM = 64
ATT_DIM = ATT_HEADS * ATT_HEAD_DIM
DILATION_PATTERNS = ((128, 1), (512, 4), (2048, 16))
ATT_MAX_WINDOW = 2048
ATT_KEYS = DILATION_PATTERNS[0][0] // DILATION_PATTERNS[0][1] + 1
ATT_Q_BLOCK = 64
D_MIX = SSD_INNER + GLA_DV + ATT_DIM
IN_SPLITS = (SSD_INNER, SSD_CONV_DIM, SSD_HEADS,
             GLA_DK, GLA_DK, GLA_DV, GLA_DV, GLA_GATE_RANK,
             ATT_DIM, ATT_DIM, ATT_DIM)
D_IN_PROJ = sum(IN_SPLITS)
D_FF = ((8 * D_MODEL // 3 + 127) // 128) * 128
ADALN_MODS = 9
FFN_RES = 0.5
EPS = 1e-6

kernel_name = 'hybrid_ssd_gla_dilated_macaron_adaln_step'

def rmsnorm(x, w):
    xf = x.astype(jnp.float32)
    y = xf * lax.rsqrt(jnp.mean(xf * xf, axis=-1, keepdims=True) + EPS)
    return (y * w.astype(jnp.float32)).astype(x.dtype)

def modulate(h, shift, scale):
    return h * (1.0 + scale) + shift

def split_cols(h, sizes):
    offs = [int(o) for o in np.cumsum(sizes)[:-1]]
    return jnp.split(h, offs, axis=-1)

def swiglu(h, w_in, w_out):
    gate, up = jnp.split(h @ w_in, 2, axis=-1)
    return (jax.nn.silu(gate) * up) @ w_out

def causal_depthwise_conv(u, buf, w, b):
    full = jnp.concatenate([buf.astype(u.dtype), u], axis=1)
    out = lax.conv_general_dilated(full, w[:, None, :].astype(u.dtype), window_strides=(1,), padding='VALID',
                                   dimension_numbers=('NWC', 'WIO', 'NWC'), feature_group_count=u.shape[-1])
    return out + b, full[:, full.shape[1] - (SSD_CONV - 1):]

def ssd_chunked(x, dt, A, Bm, Cm, h0):
    f32 = jnp.float32
    Bsz, L, H, P = x.shape
    G, N = Bm.shape[2], Bm.shape[3]
    R = H // G
    Q = SSD_CHUNK if L % SSD_CHUNK == 0 else L
    nc = L // Q
    xc = x.astype(f32).reshape(Bsz, nc, Q, G, R, P)
    dtc = dt.reshape(Bsz, nc, Q, G, R)
    Bc = Bm.astype(f32).reshape(Bsz, nc, Q, G, N)
    Cc = Cm.astype(f32).reshape(Bsz, nc, Q, G, N)
    cum = jnp.cumsum(dtc * A.reshape(G, R), axis=2)
    cumT = jnp.moveaxis(cum, 2, -1)
    causal = jnp.tril(jnp.ones((Q, Q), bool))
    decay = jnp.exp(jnp.where(causal, cumT[..., :, None] - cumT[..., None, :], -jnp.inf))
    xdt = xc * dtc[..., None]
    cb = jnp.einsum('bcqgn,bcsgn->bcgqs', Cc, Bc)
    y_diag = jnp.einsum('bcgrqs,bcsgrp->bcqgrp', cb[:, :, :, None] * decay, xdt)
    to_end = jnp.exp(cum[:, :, -1:] - cum)
    s_local = jnp.einsum('bcsgn,bcsgrp->bcgrpn', Bc, xdt * to_end[..., None])
    chunk_decay = jnp.exp(cum[:, :, -1])

    def step(h, inp):
        dec, s = inp
        return dec[..., None, None] * h + s, h

    h_last, h_in = lax.scan(step, h0.astype(f32).reshape(Bsz, G, R, P, N),
                            (jnp.moveaxis(chunk_decay, 1, 0), jnp.moveaxis(s_local, 1, 0)))
    h_in = jnp.moveaxis(h_in, 0, 1)
    y_off = jnp.einsum('bcqgn,bcgrpn->bcqgrp', Cc, h_in) * jnp.exp(cum)[..., None]
    return (y_diag + y_off).reshape(Bsz, L, H, P), h_last.reshape(Bsz, H, P, N)

def gla_chunked(q, k, v, g, S0):
    f32 = jnp.float32
    Bsz, L, H, K = q.shape
    V = v.shape[-1]
    Q = GLA_CHUNK if L % GLA_CHUNK == 0 else L
    nc = L // Q
    qc = q.astype(f32).reshape(Bsz, nc, Q, H, K)
    kc = k.astype(f32).reshape(Bsz, nc, Q, H, K)
    vc = v.astype(f32).reshape(Bsz, nc, Q, H, V)
    Gc = jnp.cumsum(g.reshape(Bsz, nc, Q, H, K), axis=2)
    causal = jnp.tril(jnp.ones((Q, Q), bool))
    dec = jnp.exp(jnp.where(causal[:, :, None, None], Gc[:, :, :, None] - Gc[:, :, None], -jnp.inf))
    att = jnp.einsum('bctshk,bcshk->bchts', qc[:, :, :, None] * dec, kc)
    o_intra = jnp.einsum('bchts,bcshv->bcthv', att, vc)
    s_local = jnp.einsum('bcshk,bcshv->bchkv', kc * jnp.exp(Gc[:, :, -1:] - Gc), vc)
    chunk_decay = jnp.exp(Gc[:, :, -1])

    def step(S, inp):
        dec_c, s = inp
        return dec_c[..., None] * S + s, S

    S_last, S_in = lax.scan(step, S0.astype(f32), (jnp.moveaxis(chunk_decay, 1, 0), jnp.moveaxis(s_local, 1, 0)))
    S_in = jnp.moveaxis(S_in, 0, 1)
    o_inter = jnp.einsum('bcthk,bchkv->bcthv', qc * jnp.exp(Gc), S_in)
    return (o_intra + o_inter).reshape(Bsz, L, H, V), S_last

def dilated_attention(q, k_ctx, v_ctx, n_buf, n_abs):
    f32 = jnp.float32
    Bsz, L, H, Dh = q.shape
    pad = ((0, 0), (ATT_MAX_WINDOW, 0), (0, 0), (0, 0))
    kp = jnp.pad(k_ctx, pad)
    vp = jnp.pad(v_ctx, pad)
    qb = ATT_Q_BLOCK if L % ATT_Q_BLOCK == 0 else L
    nb = L // qb
    strides = jnp.array([d for _, d in DILATION_PATTERNS], jnp.int32)
    dist = strides[:, None] * jnp.arange(ATT_KEYS, dtype=jnp.int32)[None, :]
    scale = ATT_HEAD_DIM ** -0.5

    def block(bi):
        i = bi * qb + jnp.arange(qb, dtype=jnp.int32)
        idx = ATT_MAX_WINDOW + n_buf + i[None, :, None] - dist[:, None, :]
        valid = dist[:, None, :] <= n_abs + i[None, :, None]
        kg = kp[:, idx]
        vg = vp[:, idx]
        qblk = lax.dynamic_slice_in_dim(q, bi * qb, qb, axis=1)
        s = jnp.einsum('bqhd,bpqjhd->bpqhj', qblk, kg).astype(f32) * scale
        s = jnp.where(valid[:, :, None, :], s, -jnp.inf)
        lse = jax.nn.logsumexp(s, axis=-1)
        p = jnp.exp(s - lse[..., None])
        o = jnp.einsum('bpqhj,bpqjhd->bpqhd', p.astype(vg.dtype), vg).astype(f32)
        w = jax.nn.softmax(lse, axis=1)
        return jnp.einsum('bpqh,bpqhd->bqhd', w, o).astype(q.dtype)

    out = lax.map(block, jnp.arange(nb, dtype=jnp.int32))
    return jnp.moveaxis(out, 0, 1).reshape(Bsz, L, H, Dh)

def token_mixers(h, st_ssd, st_conv, st_gla, k_buf, v_buf, n_abs, keep, lp):
    f32 = jnp.float32
    Bsz, L, _ = h.shape
    proj = h @ lp['w_in']
    z, xbc, dt_raw, gq, gk, gv, gr, g_lr, aq, ak, av = split_cols(proj, IN_SPLITS)
    xbc_c, conv_new = causal_depthwise_conv(xbc, st_conv, lp['ssd_conv_w'], lp['ssd_conv_b'])
    xbc_c = jax.nn.silu(xbc_c)
    xs, bs, cs = split_cols(xbc_c, (SSD_INNER, SSD_GROUPS * SSD_STATE, SSD_GROUPS * SSD_STATE))
    xs = xs.reshape(Bsz, L, SSD_HEADS, SSD_HEAD_DIM)
    dt = jax.nn.softplus(dt_raw.astype(f32) + lp['ssd_dt_bias'].astype(f32))
    A = -jnp.exp(lp['ssd_a_log'].astype(f32))
    y, ssd_new = ssd_chunked(xs, dt, A, bs.reshape(Bsz, L, SSD_GROUPS, SSD_STATE),
                             cs.reshape(Bsz, L, SSD_GROUPS, SSD_STATE), st_ssd)
    y = y + lp['ssd_d'].astype(f32)[:, None] * xs.astype(f32)
    y = y.reshape(Bsz, L, SSD_INNER) * jax.nn.silu(z.astype(f32))
    y = rmsnorm(y.reshape(Bsz, L, SSD_GROUPS, SSD_INNER // SSD_GROUPS),
                lp['ssd_norm_w'].reshape(SSD_GROUPS, SSD_INNER // SSD_GROUPS)).reshape(Bsz, L, SSD_INNER).astype(h.dtype)
    q = gq.reshape(Bsz, L, GLA_HEADS, GLA_HEAD_K) * (GLA_HEAD_K ** -0.5)
    k = gk.reshape(Bsz, L, GLA_HEADS, GLA_HEAD_K)
    v = gv.reshape(Bsz, L, GLA_HEADS, GLA_HEAD_V)
    glog = jax.nn.log_sigmoid((g_lr @ lp['gla_w_gate'] + lp['gla_b_gate']).astype(f32)) / GLA_TAU
    o, gla_new = gla_chunked(q, k, v, glog.reshape(Bsz, L, GLA_HEADS, GLA_HEAD_K), st_gla)
    o = rmsnorm(o, lp['gla_norm_w']) * jax.nn.silu(gr.astype(f32)).reshape(Bsz, L, GLA_HEADS, GLA_HEAD_V)
    o = o.reshape(Bsz, L, GLA_DV).astype(h.dtype)
    aq = aq.reshape(Bsz, L, ATT_HEADS, ATT_HEAD_DIM)
    ak = ak.reshape(Bsz, L, ATT_HEADS, ATT_HEAD_DIM)
    av = av.reshape(Bsz, L, ATT_HEADS, ATT_HEAD_DIM)
    k_ctx = jnp.concatenate([k_buf.astype(ak.dtype), ak], axis=1)
    v_ctx = jnp.concatenate([v_buf.astype(av.dtype), av], axis=1)
    att = dilated_attention(aq, k_ctx, v_ctx, k_buf.shape[1], n_abs).reshape(Bsz, L, ATT_DIM).astype(h.dtype)
    mix = jnp.concatenate([y, o, att], axis=-1) @ lp['w_out']
    new_state = (ssd_new.astype(h.dtype), conv_new, gla_new.astype(h.dtype), ak[:, L - keep:], av[:, L - keep:])
    return mix, new_state

def run_trunk(x, c, st_ssd, st_conv, st_gla, k_buf, v_buf, n_abs, keep, params, norm_f):
    outs = ([], [], [], [], [])
    for l in range(DEPTH):
        lp = {name: arr[l] for name, arr in params.items()}
        mod = (jax.nn.silu(c) @ lp['w_mod'] + lp['b_mod']).reshape(c.shape[0], ADALN_MODS, 1, D_MODEL)
        h = modulate(rmsnorm(x, lp['norm_w'][0]), mod[:, 0], mod[:, 1])
        x = x + FFN_RES * mod[:, 2] * swiglu(h, lp['ffn1_w_in'], lp['ffn1_w_out'])
        h = modulate(rmsnorm(x, lp['norm_w'][1]), mod[:, 3], mod[:, 4])
        mix, new = token_mixers(h, st_ssd[l], st_conv[l], st_gla[l], k_buf[l], v_buf[l], n_abs, keep, lp)
        x = x + mod[:, 5] * mix
        h = modulate(rmsnorm(x, lp['norm_w'][2]), mod[:, 6], mod[:, 7])
        x = x + FFN_RES * mod[:, 8] * swiglu(h, lp['ffn2_w_in'], lp['ffn2_w_out'])
        for acc, s in zip(outs, new):
            acc.append(s)
    return rmsnorm(x, norm_f), [jnp.stack(acc) for acc in outs]

def setup_inputs(seed: int = 0) -> dict:
    key = jax.random.key(seed)
    ks = iter(jax.random.split(key, 40))
    f32 = jnp.float32

    def nrm(shape, scale):
        return jax.random.normal(next(ks), shape, f32) * scale

    win_buf = min(ATT_MAX_WINDOW, PAST_LEN)
    dt0 = jnp.exp(jax.random.uniform(next(ks), (DEPTH, SSD_HEADS), f32, math.log(1e-3), math.log(1e-1)))
    ssd_dt_bias = dt0 + jnp.log(-jnp.expm1(-dt0))
    ssd_a_log = jnp.log(jax.random.uniform(next(ks), (DEPTH, SSD_HEADS), f32, 1.0, 16.0))
    return {
        'x_prompt': nrm((BATCH, SEQ, D_MODEL), 1.0),
        'x_sample': nrm((DEC_BATCH, DEC_SEQ, D_MODEL), 1.0),
        'c_prompt': nrm((BATCH, D_MODEL), 1.0),
        'c_sample': nrm((DEC_BATCH, D_MODEL), 1.0),
        'state_ssd': nrm((DEPTH, DEC_BATCH, SSD_HEADS, SSD_HEAD_DIM, SSD_STATE), 0.1),
        'state_ssd_conv': nrm((DEPTH, DEC_BATCH, SSD_CONV - 1, SSD_CONV_DIM), 1.0),
        'state_gla': nrm((DEPTH, DEC_BATCH, GLA_HEADS, GLA_HEAD_K, GLA_HEAD_V), 1.0),
        'cache_attn_k': nrm((DEPTH, DEC_BATCH, win_buf, ATT_HEADS, ATT_HEAD_DIM), 1.0),
        'cache_attn_v': nrm((DEPTH, DEC_BATCH, win_buf, ATT_HEADS, ATT_HEAD_DIM), 1.0),
        'w_in': nrm((DEPTH, D_MODEL, D_IN_PROJ), D_MODEL ** -0.5),
        'w_out': nrm((DEPTH, D_MIX, D_MODEL), D_MIX ** -0.5),
        'ssd_conv_w': nrm((DEPTH, SSD_CONV, SSD_CONV_DIM), SSD_CONV ** -0.5),
        'ssd_conv_b': nrm((DEPTH, SSD_CONV_DIM), 0.02),
        'ssd_dt_bias': ssd_dt_bias,
        'ssd_a_log': ssd_a_log,
        'ssd_d': 1.0 + nrm((DEPTH, SSD_HEADS), 0.1),
        'ssd_norm_w': 1.0 + nrm((DEPTH, SSD_INNER), 0.1),
        'gla_w_gate': nrm((DEPTH, GLA_GATE_RANK, GLA_DK), GLA_GATE_RANK ** -0.5),
        'gla_b_gate': nrm((DEPTH, GLA_DK), 0.1),
        'gla_norm_w': 1.0 + nrm((DEPTH, GLA_HEAD_V), 0.1),
        'norm_w': 1.0 + nrm((DEPTH, 3, D_MODEL), 0.1),
        'w_mod': nrm((DEPTH, D_MODEL, ADALN_MODS * D_MODEL), 0.5 * D_MODEL ** -0.5),
        'b_mod': nrm((DEPTH, ADALN_MODS * D_MODEL), 0.02),
        'ffn1_w_in': nrm((DEPTH, D_MODEL, 2 * D_FF), D_MODEL ** -0.5),
        'ffn1_w_out': nrm((DEPTH, D_FF, D_MODEL), D_FF ** -0.5),
        'ffn2_w_in': nrm((DEPTH, D_MODEL, 2 * D_FF), D_MODEL ** -0.5),
        'ffn2_w_out': nrm((DEPTH, D_FF, D_MODEL), D_FF ** -0.5),
        'norm_f': 1.0 + nrm((D_MODEL,), 0.1),
    }

def reference(x_prompt, x_sample, c_prompt, c_sample, state_ssd, state_ssd_conv, state_gla, cache_attn_k, cache_attn_v,
              w_in, w_out, ssd_conv_w, ssd_conv_b, ssd_dt_bias, ssd_a_log, ssd_d, ssd_norm_w,
              gla_w_gate, gla_b_gate, gla_norm_w, norm_w, w_mod, b_mod,
              ffn1_w_in, ffn1_w_out, ffn2_w_in, ffn2_w_out, norm_f):
    params = dict(w_in=w_in, w_out=w_out, ssd_conv_w=ssd_conv_w, ssd_conv_b=ssd_conv_b, ssd_dt_bias=ssd_dt_bias,
                  ssd_a_log=ssd_a_log, ssd_d=ssd_d, ssd_norm_w=ssd_norm_w, gla_w_gate=gla_w_gate,
                  gla_b_gate=gla_b_gate, gla_norm_w=gla_norm_w, norm_w=norm_w, w_mod=w_mod, b_mod=b_mod,
                  ffn1_w_in=ffn1_w_in, ffn1_w_out=ffn1_w_out, ffn2_w_in=ffn2_w_in, ffn2_w_out=ffn2_w_out)
    dtp = x_prompt.dtype
    p_ssd0 = jnp.zeros((DEPTH, BATCH, SSD_HEADS, SSD_HEAD_DIM, SSD_STATE), dtp)
    p_conv0 = jnp.zeros((DEPTH, BATCH, SSD_CONV - 1, SSD_CONV_DIM), dtp)
    p_gla0 = jnp.zeros((DEPTH, BATCH, GLA_HEADS, GLA_HEAD_K, GLA_HEAD_V), dtp)
    p_kv0 = jnp.zeros((DEPTH, BATCH, 0, ATT_HEADS, ATT_HEAD_DIM), dtp)
    y_prompt, (ssd_p, conv_p, gla_p, k_p, v_p) = run_trunk(
        x_prompt, c_prompt, p_ssd0, p_conv0, p_gla0, p_kv0, p_kv0, 0, min(ATT_MAX_WINDOW, SEQ), params, norm_f)
    y_sample, (ssd_s, conv_s, gla_s, k_s, v_s) = run_trunk(
        x_sample, c_sample, state_ssd, state_ssd_conv, state_gla, cache_attn_k, cache_attn_v,
        PAST_LEN, DEC_SEQ, params, norm_f)
    return (y_prompt, y_sample, ssd_p, ssd_s, conv_p, conv_s, gla_p, gla_s, k_p, k_s, v_p, v_s)


_drawn_inputs = setup_inputs


def setup_inputs(seed=0):
    import zlib

    import numpy as np

    out = dict(_drawn_inputs(seed))
    spreads = {}
    factors = {'ssd_d': 7.805, 'gla_norm_w': 4.204}
    for name, (base, spread) in spreads.items():
        noise = np.random.default_rng([zlib.crc32(name.encode()), seed]).standard_normal(out[name].shape)
        drawn = base * np.exp(spread * noise) if base else spread * noise
        out[name] = jnp.asarray(drawn.astype(out[name].dtype))
    for name, factor in factors.items():
        out[name] = (out[name] * factor).astype(out[name].dtype)
    return out
```

```python
import math
from contextlib import ExitStack

import concourse.bass as bass
from concourse import mybir

F32 = mybir.dt.float32
I32 = mybir.dt.int32
ALU = mybir.AluOpType
ACT = mybir.ActivationFunctionType
AX = mybir.AxisListType

D = 1024
DEPTH = 2
SEQ = 512
NB, NI = 8, 8
TS = NB * NI
T = SEQ + TS
HALF = T // 2
P = 128
DT = D // P
NSEQ = 1 + NB
FF = ((8 * D // 3 + 127) // 128) * 128
FT = FF // P
PAST = 256
EPS = 1e-6

SH, SP_, SN, SG = 6, 64, 128, 2
SI = SH * SP_
CONV = 4
CT = (SI + 2 * SG * SN) // P
GH, GK, GV = 4, 32, 64
GDV = GH * GV
RANK = 16
TAU = 16.0
AH, AD = 6, 64
AI = AH * AD
NJ = AH * AD // P
NCH = SEQ // P
NTT = NCH + 1
NEG = -1e30

splits = (SI, CT * P, SH, GH * GK, GH * GK, GDV, GDV, RANK, AI, AI, AI)
(O_Z, O_XBC, O_DT, O_GQ, O_GK, O_GV, O_GR, O_LR, O_AQ, O_AK, O_AV) = [sum(splits[:i]) for i in range(11)]
D_IN = sum(splits)

R_BMOD, R_NORM, R_CONVB, R_SNORM, R_BGATE, R_GNORM = 0, 72, 96, 103, 106, 107
N_PROW = 108

SLOT = FT * P
U_FF1 = 0
U_FO1 = U_FF1 + FT
U_IN = U_FO1 + DT
IN_UNITS = [("aqk", O_AQ, 256), ("aqk", O_AQ + 256, 256), ("aqk", O_AQ + 512, 256),
            ("av", O_AV, 192), ("av", O_AV + 192, 192),
            ("gqk", O_GQ, 256), ("gr", O_GR, 272), ("gv", O_GV, 256),
            ("zx", 0, 256), ("zx", 256, 256), ("zx", 512, 256), ("zx", 768, 256), ("zx", 1024, 262)]
U_OUT = U_IN + len(IN_UNITS)
U_FF2 = U_OUT + 4
U_FO2 = U_FF2 + FT
U_END = U_FO2 + DT
ARENA = 31500


def projection_groups():
    out = []
    for u, (kind, c0, width) in enumerate(IN_UNITS):
        nth = sum(1 for k, _, _ in IN_UNITS[:u] if k == kind)
        if kind in ("av", "gv"):
            out += [(u, kind, "token", t, nth) for t in range(NTT)]
            continue
        out += [(u, kind, "feature", c, 2 * nth + c) for c in range(2)]
        if kind == "gr":
            out.append((u, "lr", "feature", 2, 0))
        if c0 + width == O_DT + SH:
            out += [(u, "dt", "token", t, 0) for t in range(NTT)]
    return out


GROUPS = projection_groups()


def groups_after(n):
    if n < U_IN:
        return n + 1
    if n < U_OUT:
        return U_IN + sum(1 for g in GROUPS if g[0] <= n - U_IN)
    done = U_IN + len(GROUPS)
    if n < U_FF2:
        return done + 2 * (n - U_OUT + 1)
    return done + DT + n - U_FF2 + 1


def program(nc, A, O):
    ctx = ExitStack()
    with ctx:
        def sb(name, shape, dt=F32):
            return ctx.enter_context(nc.sbuf_tensor(name, shape, dt))

        w_ready = [ctx.enter_context(nc.semaphore(f"w_ready{k}")) for k in range(2)]
        group_done = ctx.enter_context(nc.semaphore("group_done"))
        stage_ctx, stage_sems = ExitStack(), {}

        def sem(name):
            if name not in stage_sems:
                stage_sems[name] = stage_ctx.enter_context(nc.semaphore(name))
            return stage_sems[name]

        def end_stage(also=()):
            with nc.Block(no_gpsimd_drain=True) as block:
                @block.sync
                def _(e):
                    for s in list(stage_sems.values()) + list(also):
                        e.sem_clear(s)
            stage_ctx.close()
            stage_sems.clear()

        xT = sb("xT", [P, DT, T])
        hT = sb("hT", [P, DT, T])
        modT = sb("modT", [P, 72, NSEQ])
        modA = sb("modA", [P, 3, DT, NSEQ])
        cT = sb("cT", [P, DT, NSEQ])
        cols = sb("cols", [P, N_PROW])
        convw = sb("convw", [P, CONV * CT])
        wslot = sb("wslot", [P, 2, SLOT])
        ident = sb("ident", [P, P])
        ones = sb("ones", [P, P])
        tri = sb("tri", [P, P])
        gts = sb("gts", [P, P])
        tri8 = sb("tri8", [TS, TS])
        gt8 = sb("gt8", [TS, TS])
        bsel = sb("bsel", [TS, NB])
        bd64 = sb("bd64", [P, P])
        hmask = sb("hmask", [P, GDV])
        levm = sb("levm", [P, 8, P])
        nwin = sb("nwin", [P, SEQ])
        ndec = sb("ndec", [P, PAST + TS])
        rmask = sb("rmask", [P, T])
        normf = sb("normf", [P, DT])
        epsc = sb("epsc", [P, 1])
        rms = sb("rms", [P, T])
        small = sb("small", [P, T])

        arena = sb("arena", [P, ARENA])
        PS = ctx.enter_context(nc.psum_tensor("PS", [P, 8, 512], F32))

        def carve(sizes, start=0):
            out, at = [], start
            for shape in sizes:
                n = 1
                for s in shape:
                    n *= s
                v = arena[:, at:at + n]
                if len(shape) == 2:
                    v = v.rearrange("p (a b) -> p a b", a=shape[0])
                elif len(shape) == 3:
                    v = v.rearrange("p (a b c) -> p a b c", a=shape[0], b=shape[1])
                out.append(v)
                at += n
            assert at <= ARENA, at
            return out, at

        (act, sg), _ = carve([(FT, T), (2, T)])
        (zT, U, Us, dtr, gqT, gkT, glr, grT, gv, aqT, akT, av), SCR = carve(
            [(3, T), (CT, SEQ + 3), (CT, NB, NI + 3), (NTT, SH), (1, T), (1, T), (1, T), (2, T),
             (NTT, GDV), (NJ, T), (NJ, T), (NTT, AI)])
        gqT, gkT, glr = gqT[:, 0, :], gkT[:, 0, :], glr[:, 0, :]

        SSD_SCR = 3 * T + CT * (SEQ + 3) + CT * NB * (NI + 3) + NTT * SH
        ATT_IN = SCR - 2 * NJ * T - NTT * AI

        def bc(ap, axis, n):
            v = ap.unsqueeze(axis)
            shape = list(v.shape)
            shape[axis] = n
            return v.to_broadcast(shape)

        def absolute(e, out, x):
            return e.scalar_tensor_tensor(out=out, in0=x, scalar=-1.0, in1=x, op0=ALU.mult, op1=ALU.max)

        def halves(ap):
            return ap.rearrange("p (h n) -> p h n", h=2)

        def bank2(b):
            return PS[:, b:b + 2, 0:HALF]

        def dram_rows(ap, l, rows=None):
            v = ap[bass.ds(l, 1)]
            return v.rearrange("a (k p) n -> p (a k) n", p=P)

        def load_unit(e, l, n, i=0):
            k = n % 2
            first = n < 2 and isinstance(i, int) and i == 0
            if not first:
                e.wait_ge(group_done, groups_after(n - 2) + 2 * i)
            slot = wslot[:, k, :]
            if U_FF1 <= n < U_FO1 or U_FF2 <= n < U_FO2:
                w = A["ffn1_w_in"] if n < U_FO1 else A["ffn2_w_in"]
                f = (n - (U_FF1 if n < U_FO1 else U_FF2)) + 2 * i
                v = dram_rows(w, l).rearrange("p k (g n) -> p k g n", g=2)
                dst = slot[:, 0:DT * 2 * P].rearrange("p (g k n) -> p g k n", k=DT, g=2)
                for g in range(2):
                    e.dma_start(dst[:, g], v[:, :, g, bass.ds(f * P, P)]).then_inc(w_ready[k], 16)
            elif U_FO1 <= n < U_IN or U_FO2 <= n < U_END:
                w = A["ffn1_w_out"] if n < U_IN else A["ffn2_w_out"]
                d = (n - (U_FO1 if n < U_IN else U_FO2)) + 2 * i
                v = dram_rows(w, l)
                dst = slot[:, 0:FT * P].rearrange("p (k n) -> p k n", k=FT)
                for a, b in ((0, FT // 2), (FT // 2, FT)):
                    e.dma_start(dst[:, a:b], v[:, a:b, bass.ds(d * P, P)]).then_inc(w_ready[k], 16)
            else:
                if n < U_OUT:
                    _, c0, w = IN_UNITS[n - U_IN]
                    v = dram_rows(A["w_in"], l)
                else:
                    c0, w = (n - U_OUT) * 256, 256
                    v = dram_rows(A["w_out"], l)
                dst = slot[:, 0:DT * w].rearrange("p (k n) -> p k n", k=DT)
                for a, b in ((0, 4), (4, 8)):
                    e.dma_start(dst[:, a:b], v[:, a:b, c0:c0 + w]).then_inc(w_ready[k], 16)

        def load_units(e, l, a, b):
            n = a
            for lo, hi in ((U_FF1, U_FO1), (U_FO1, U_IN), (U_IN, U_FF2), (U_FF2, U_FO2), (U_FO2, U_END)):
                end = min(b, hi)
                if n >= end or n < lo:
                    continue
                if (lo, hi) == (U_IN, U_FF2):
                    for m in range(n, end):
                        load_unit(e, l, m)
                    n = end
                    continue
                if n < 2:
                    load_unit(e, l, n)
                    load_unit(e, l, n + 1)
                    n += 2
                pairs = (end - n) // 2
                if pairs > 1:
                    with e.Fori(0, pairs) as i:
                        load_unit(e, l, n, i)
                        load_unit(e, l, n + 1, i)
                    n += 2 * pairs
                for m in range(n, end):
                    load_unit(e, l, m)
                n = end

        def wait_unit(e, n, i=0):
            e.wait_ge(w_ready[n % 2], 32 * (n // 2 + 1) + 32 * i)

        class Link:

            def __init__(self, e, name):
                self.e, self.s, self.n = e, sem(name), 0

            def __call__(self, ins):
                self.n += 1
                ins.then_inc(self.s, 1)
                self.e.wait_ge(self.s, self.n)

        with ExitStack() as st:
            (xin, cin, nfr, mtmp, mdd, dd, ipart, icol, idist, irow, idec, itmp), _ = carve(
                [(NTT, D), (1, D), (1, P), (1, SEQ), (1, SEQ), (1, PAST + TS), (1, P), (1, P), (1, SEQ), (1, 2),
                 (1, PAST + TS), (1, SEQ)])
            cin, nfr, mtmp, mdd, dd = cin[:, 0, :], nfr[:, 0, :], mtmp[:, 0, :], mdd[:, 0, :], dd[:, 0, :]
            ipart, icol, idist, irow, idec, itmp = [v[:, 0, :].bitcast(I32)
                                                    for v in (ipart, icol, idist, irow, idec, itmp)]
            s_in, s_cin, s_masks = sem("x_loaded"), sem("c_loaded"), sem("pool_step")
            s_tp, s_xs, s_xp = sem("x_turned"), sem("xs_kept"), sem("xp_kept")
            s_cs, s_ct, s_iota = sem("c_silu"), sem("c_turned"), sem("iota_ready")
            N_MASKS = 17
            block = st.enter_context(nc.Block())

            @block.sync
            def _(e):
                for t in range(NCH):
                    e.dma_start(xin[:, t, :], A["x_prompt"][0, t * P:(t + 1) * P, :]).then_inc(s_in, 16)
                e.dma_start(xin[0:TS, NCH, :], A["x_sample"].rearrange("b i d -> (b i) d")).then_inc(s_in, 16)

            @block.gpsimd
            def _(e):
                link = Link(e, "pool_step")
                link(e.memset(ident[:], 0.0))
                link(e.memset(ones[:], 1.0))
                link(e.memset(bd64[:], 0.0))
                link(e.memset(bd64[0:64, 0:64], 1.0))
                link(e.memset(bd64[64:P, 64:P], 1.0))
                link(e.memset(bsel[:], 1.0))
                link(e.memset(hmask[:], 0.0))
                for h in range(GH):
                    link(e.memset(hmask[h * GK:(h + 1) * GK, h * GV:(h + 1) * GV], 1.0))
                link(e.affine_select(out=ident[:], in_=ident[:], compare_op=ALU.not_equal, fill=1.0,
                                     base=0, pattern=[[-1, P]], channel_multiplier=1))
                link(e.affine_select(out=tri[:], in_=ones[:], compare_op=ALU.is_ge, fill=0.0,
                                     base=0, pattern=[[1, P]], channel_multiplier=-1))
                link(e.affine_select(out=gts[:], in_=ones[:], compare_op=ALU.is_gt, fill=0.0,
                                     base=0, pattern=[[-1, P]], channel_multiplier=1))
                link(e.affine_select(out=bsel[:], in_=bsel[:], compare_op=ALU.is_ge, fill=0.0,
                                     base=0, pattern=[[-NI, NB]], channel_multiplier=1))
                link(e.affine_select(out=bsel[:], in_=bsel[:], compare_op=ALU.is_gt, fill=0.0,
                                     base=NI, pattern=[[NI, NB]], channel_multiplier=-1))
                link(e.memset(rmask[:], 1.0))
                e.iota(ipart, [[0, P]], base=0, channel_multiplier=1).then_inc(s_iota, 1)
                e.iota(icol, [[1, P]], base=0, channel_multiplier=0).then_inc(s_iota, 1)
                e.iota(idist, [[-1, SEQ]], base=SEQ - P, channel_multiplier=1).then_inc(s_iota, 1)
                e.iota(idec[:, 0:PAST], [[-1, PAST]], base=PAST, channel_multiplier=0).then_inc(s_iota, 1)
                e.iota(idec[:, PAST:PAST + TS], [[1, TS]], base=0, channel_multiplier=0).then_inc(s_iota, 1)

            @block.scalar
            def _(e):
                e.dma_start(cin[0:1, :], A["c_prompt"]).then_inc(s_cin, 16)
                e.dma_start(cin[1:NSEQ, :], A["c_sample"]).then_inc(s_cin, 16)
                e.dma_start(nfr[0:DT, :], A["norm_f"].rearrange("(a p) -> a p", p=P)).then_inc(s_cin, 16)
                e.wait_ge(s_cin, 48)
                e.activation(cin[0:NSEQ, :], cin[0:NSEQ, :], ACT.Silu).then_inc(s_cs, 1)
                for d in range(DT):
                    e.wait_ge(s_tp, d + 1)
                    e.activation(xT[:, d, SEQ:T], PS[:, 2 * (d % 2) + 1, 0:TS], ACT.Copy).then_inc(s_xs, 1)

            @block.tensor
            def _(e):
                e.wait_ge(s_in, 16 * NTT)
                e.wait_ge(s_masks, N_MASKS)
                for d in range(DT):
                    if d >= 2:
                        e.wait_ge(s_xs, d - 1)
                        e.wait_ge(s_xp, d - 1)
                    b = 2 * (d % 2)
                    for t in range(NCH):
                        e.transpose(PS[:, b, t * P:(t + 1) * P], xin[:, t, d * P:(d + 1) * P], ident[:])
                    e.transpose(PS[:, b + 1, 0:TS], xin[0:TS, NCH, d * P:(d + 1) * P], ident[0:TS, 0:TS])\
                        .then_inc(s_tp, 1)
                e.wait_ge(s_cs, 1)
                for d in range(DT):
                    e.transpose(PS[:, 4, d * NSEQ:(d + 1) * NSEQ], cin[0:NSEQ, d * P:(d + 1) * P],
                                ident[0:NSEQ, 0:NSEQ])
                e.transpose(PS[:, 4, DT * NSEQ:DT * NSEQ + DT], nfr[0:DT, :], ident[0:DT, 0:DT]).then_inc(s_ct, 1)

            @block.vector
            def _(e):
                link = Link(e, "dve_step")
                e.memset(epsc[:], EPS)
                e.wait_ge(s_masks, N_MASKS)
                e.wait_ge(s_iota, 5)
                link(e.memset(rmask[:, 0:SEQ:P], 0.0))
                link(e.memset(rmask[:, SEQ:T:NI], 0.0))
                for d in range(DT):
                    e.wait_ge(s_tp, d + 1)
                    e.tensor_copy(xT[:, d, 0:SEQ], PS[:, 2 * (d % 2), :]).then_inc(s_xp, 1)
                e.wait_ge(s_ct, 1)
                e.tensor_copy(cT[:], PS[:, 4, 0:DT * NSEQ].rearrange("p (d s) -> p d s", s=NSEQ))
                e.tensor_copy(normf[:], PS[:, 4, DT * NSEQ:DT * NSEQ + DT])

                itx = itmp[:, 0:P]
                xf, t0, t1 = mtmp[:, 0:P], mtmp[:, P:2 * P], mtmp[:, 2 * P:3 * P]
                link(e.tensor_tensor(itx, ipart, icol, ALU.bitwise_xor))
                link(e.tensor_copy(xf, itx))
                e.tensor_copy(levm[:, 0, :], ident[:])
                for k in range(7):
                    link(e.tensor_scalar(t0, xf, float(2 ** k), None, ALU.is_ge))
                    link(e.tensor_scalar(t1, xf, float(2 ** (k + 1)), None, ALU.is_lt))
                    link(e.tensor_tensor(t0, t0, t1, ALU.mult))
                    link(e.tensor_tensor(levm[:, 1 + k, :], t0, tri[:], ALU.mult))
                link(e.tensor_scalar(t0, xf, float(NI), None, ALU.is_lt))
                link(e.tensor_tensor(tri8[:], tri[0:TS, 0:TS], t0[0:TS, 0:TS], ALU.mult))
                link(e.tensor_tensor(gt8[:], gts[0:TS, 0:TS], t0[0:TS, 0:TS], ALU.mult))

                def minus_log_multiplicity(out, dist, n):
                    m, t, it = mdd[:, 0:n], mtmp[:, 0:n], itmp[:, 0:n]
                    link(e.tensor_copy(m, dist))
                    link(e.tensor_scalar(out, m, 128.0, None, ALU.is_le))
                    for stride in (4, 16):
                        link(e.tensor_scalar(it, dist, stride - 1, None, ALU.bitwise_and))
                        link(e.tensor_copy(t, it))
                        link(e.tensor_scalar(t, t, 0.0, None, ALU.is_equal))
                        link(e.tensor_tensor(out, out, t, ALU.add))
                    link(e.tensor_scalar(t, m, 0.0, None, ALU.is_ge))
                    link(e.tensor_tensor(out, out, t, ALU.mult))
                    link(e.tensor_scalar(m, out, 2.0, -math.log(2.0), ALU.is_equal, ALU.mult))
                    link(e.tensor_scalar(t, out, 3.0, -math.log(3.0), ALU.is_equal, ALU.mult))
                    link(e.tensor_tensor(m, m, t, ALU.add))
                    link(e.tensor_scalar(t, out, 0.0, -NEG, ALU.is_equal, ALU.mult))
                    link(e.tensor_tensor(out, m, t, ALU.add))

                minus_log_multiplicity(nwin[:], idist, SEQ)
                link(e.tensor_scalar(irow[:, 0:1], ipart[:, 0:1], NI - 1, None, ALU.bitwise_and))
                link(e.tensor_scalar(irow[:, 1:2], ipart[:, 0:1], 4, None, ALU.logical_shift_right))
                row = small[:, 0:2]
                link(e.tensor_copy(row, irow))
                link(e.tensor_scalar(itmp[:, 0:TS], idec[:, PAST:PAST + TS], NI - 1, None, ALU.bitwise_and))
                link(e.tensor_copy(small[:, 64:64 + TS], itmp[:, 0:TS]))
                link(e.tensor_scalar(itmp[:, 0:TS], idec[:, PAST:PAST + TS], 3, None, ALU.logical_shift_right))
                link(e.tensor_copy(small[:, 128:128 + TS], itmp[:, 0:TS]))
                link(e.tensor_copy(dd[:, 0:PAST], idec[:, 0:PAST]))
                link(e.tensor_scalar(dd[:, 0:PAST], dd[:, 0:PAST], row[:, 0:1], None, ALU.add))
                link(e.tensor_scalar(dd[:, PAST:PAST + TS], small[:, 64:64 + TS], -1.0, row[:, 0:1],
                                     ALU.mult, ALU.add))
                link(e.tensor_scalar(small[:, 128:128 + TS], small[:, 128:128 + TS], row[:, 1:2], -1024.0,
                                     ALU.not_equal, ALU.mult))
                link(e.tensor_tensor(dd[:, PAST:PAST + TS], dd[:, PAST:PAST + TS], small[:, 128:128 + TS], ALU.add))
                link(e.tensor_copy(idec, dd))
                minus_log_multiplicity(ndec[:], idec, PAST + TS)

        end_stage()

        def mod_col(m, d, s=0, n=1):
            return modT[:, bass.ds(m * DT + d, 1), s:s + n].rearrange("p a s -> p (a s)")

        def norm_act(e, q, k):
            for d in range(DT):
                e.activation(hT[:, d, :], xT[:, d, :], ACT.Square).then_inc(sem(q + "squares"), 1)
            e.wait_ge(sem(q + "sumsq"), 1)
            e.activation(halves(rms[:]), bank2(0), ACT.Sqrt, scale=1.0 / D, bias=epsc[:])\
                .then_inc(sem(q + "root"), 1)
            if k is not None:
                for d in range(DT):
                    e.wait_ge(sem(q + "x_scaled"), d + 1)
                    e.activation(hT[:, d, 0:SEQ], hT[:, d, 0:SEQ], ACT.Identity,
                                 scale=modA[:, k, d, 0:1], bias=mod_col(3 * k, d)).then_inc(sem(q + "h_ready"), 1)

        def norm_pe(e, q):
            for d in range(DT):
                e.wait_ge(sem(q + "squares"), d + 1)
                for h in range(2):
                    ins = e.matmul(PS[:, h, 0:HALF], ones[:], halves(hT[:, d, :])[:, h, :],
                                   start=(d == 0), stop=(d == DT - 1))
            ins.then_inc(sem(q + "sumsq"), 1)

        def norm_dve(e, q, k):
            e.wait_ge(sem(q + "root"), 1)
            e.reciprocal(rms[:], rms[:]).then_inc(sem(q + "inverse"), 1)
            e.wait_ge(sem(q + "inverse"), 1)
            if k is None:
                for d in range(DT):
                    e.scalar_tensor_tensor(out=hT[:, d, :], in0=xT[:, d, :], scalar=normf[:, d:d + 1], in1=rms[:],
                                           op0=ALU.mult, op1=ALU.mult).then_inc(sem(q + "h_ready"), 1)
                return
            for d in range(DT):
                e.tensor_tensor(hT[:, d, :], xT[:, d, :], rms[:], ALU.mult).then_inc(sem(q + "x_scaled"), 1)
            e.wait_ge(sem(q + "x_scaled"), DT)
            hs = hT[:, :, SEQ:T].rearrange("p d (b i) -> p d b i", i=NI)
            e.tensor_tensor(hs, hs, bc(modA[:, k, :, 1:NSEQ], 3, NI), ALU.mult).then_inc(sem(q + "inverse"), 1)
            e.wait_ge(sem(q + "inverse"), 2)
            e.tensor_tensor(hs, hs, bc(modT[:, 3 * k * DT:(3 * k + 1) * DT, 1:NSEQ], 3, NI), ALU.add)\
                .then_inc(sem(q + "h_ready"), 1)

        def add_to_x(e, link, m, d, b, k2):
            xd = xT[:, bass.ds(d, 1), :].rearrange("p a t -> p (a t)")
            e.scalar_tensor_tensor(out=xd[:, 0:HALF], in0=PS[:, b, 0:HALF], scalar=mod_col(m, d),
                                   in1=xd[:, 0:HALF], op0=ALU.mult, op1=ALU.add)
            e.scalar_tensor_tensor(out=xd[:, HALF:SEQ], in0=PS[:, b + 1, 0:SEQ - HALF], scalar=mod_col(m, d),
                                   in1=xd[:, HALF:SEQ], op0=ALU.mult, op1=ALU.add)
            own = small[:, k2 * TS:(k2 + 1) * TS]
            gated = own.rearrange("p (b i) -> p b i", i=NI)
            ins = e.tensor_tensor(gated, PS[:, b + 1, SEQ - HALF:HALF].rearrange("p (b i) -> p b i", i=NI),
                                  bc(mod_col(m, d, 1, NB), 2, NI), ALU.mult)
            link(ins)
            return e.tensor_tensor(xd[:, SEQ:T], xd[:, SEQ:T], own, ALU.add)

        def ffn_block(l, q, k, m_gate, n_in, n_out, next_units):
            with nc.Block(no_gpsimd_drain=True) as block:
                @block.sync
                def _(e):
                    load_units(e, l, n_in + 2, next_units)

                @block.tensor
                def _(e):
                    norm_pe(e, q)
                    e.wait_ge(sem(q + "h_ready"), DT + 1)

                    def gate_up(i, k2):
                        n = n_in + k2
                        wait_unit(e, n, i)
                        if not isinstance(i, int):
                            e.wait_ge(sem(q + "act_ready"), 2 * i + k2 - 1)
                        w = wslot[:, n % 2, 0:DT * 2 * P].rearrange("p (g k n) -> p g k n", k=DT, g=2)
                        for g in range(2):
                            for kt in range(DT):
                                for h in range(2):
                                    ins = e.matmul(PS[:, 4 * k2 + 2 * g + h, 0:HALF], w[:, g, kt, :],
                                                   halves(hT[:, kt, :])[:, h, :], start=(kt == 0),
                                                   stop=(kt == DT - 1))
                        ins.then_inc(group_done, 1)

                    gate_up(0, 0)
                    gate_up(0, 1)
                    with e.Fori(1, FT // 2) as i:
                        gate_up(i, 0)
                        gate_up(i, 1)
                    e.wait_ge(sem(q + "act_ready"), FT)

                    def down(i, k2):
                        n = n_out + k2
                        wait_unit(e, n, i)
                        if not isinstance(i, int):
                            e.wait_ge(sem(q + "x_added"), 2 * i + k2 - 1)
                        w = wslot[:, n % 2, :].rearrange("p (k n) -> p k n", n=P)
                        for kt in range(FT):
                            for h in range(2):
                                ins = e.matmul(PS[:, 2 * k2 + h, 0:HALF], w[:, kt, :],
                                               halves(act[:, kt, :])[:, h, :], start=(kt == 0), stop=(kt == FT - 1))
                        ins.then_inc(group_done, 1)

                    down(0, 0)
                    down(0, 1)
                    with e.Fori(1, DT // 2) as i:
                        down(i, 0)
                        down(i, 1)

                @block.scalar
                def _(e):
                    norm_act(e, q, k)
                    e.preload_act_table(ACT.Silu)

                    def gate(i, k2):
                        e.wait_ge(group_done, groups_after(n_in + k2) + 2 * i)
                        if not isinstance(i, int):
                            e.wait_ge(sem(q + "act_ready"), 2 * i + k2 - 1)
                        e.activation(halves(sg[:, k2, :]), bank2(4 * k2), ACT.Silu)\
                            .then_inc(sem(q + "gate_ready"), 1)

                    gate(0, 0)
                    gate(0, 1)
                    with e.Fori(1, FT // 2) as i:
                        gate(i, 0)
                        gate(i, 1)

                @block.vector
                def _(e):
                    norm_dve(e, q, k)

                    def act_tile(i, k2):
                        e.wait_ge(sem(q + "gate_ready"), k2 + 1 + 2 * i)
                        out = act[:, bass.ds(2 * i + k2, 1), :].rearrange("p a (h n) -> p (a h) n", h=2)
                        e.tensor_tensor(out, bank2(4 * k2 + 2), halves(sg[:, k2, :]), ALU.mult)\
                            .then_inc(sem(q + "act_ready"), 1)

                    with e.Fori(0, FT // 2) as i:
                        act_tile(i, 0)
                        act_tile(i, 1)

                    with e.Fori(0, DT // 2) as i:
                        for k2 in range(2):
                            e.wait_ge(group_done, groups_after(n_out + k2) + 2 * i)

                            def link(ins):
                                ins.then_inc(sem(q + "gated"), 1)
                                e.wait_ge(sem(q + "gated"), k2 + 1 + 2 * i)
                            add_to_x(e, link, m_gate, 2 * i + k2, 2 * k2, k2).then_inc(sem(q + "x_added"), 1)

        with nc.Fori(0, DEPTH) as l:
            (wm, prow, crow), _ = carve([(4, DT * 256), (1, P), (1, P)])
            prow, crow = prow[:, 0, :], crow[:, 0, :]
            wm_ready = [sem(f"wm_ready{k}") for k in range(4)]
            wm_used, p_loaded, p_turned = sem("wm_used"), sem("params_loaded"), sem("params_turned")
            NM = 72 // 8
            with nc.Block(no_gpsimd_drain=True) as block:
                @block.sync
                def _(e):
                    def load(i, k):
                        v = dram_rows(A["w_mod"], l)[:, :, bass.ds((4 * i + k) * 256, 256)]
                        e.dma_start(wm[:, k, :].rearrange("p (k n) -> p k n", k=DT), v).then_inc(wm_ready[k], 16)

                    for k in range(4):
                        load(0, k)
                    with e.Fori(1, NM) as i:
                        for k in range(4):
                            e.wait_ge(wm_used, 4 * i + k - 3)
                            load(i, k)
                    load_unit(e, l, 0)
                    load_unit(e, l, 1)

                @block.tensor
                def _(e):
                    with e.Fori(0, NM) as i:
                        for k in range(4):
                            e.wait_ge(wm_ready[k], 16 * i + 16)
                            w = wm[:, k, :].rearrange("p (k n) -> p k n", k=DT)
                            for c in range(2):
                                out = PS[:, 0:3, :].rearrange("p b n -> p (b n)")[
                                    :, bass.ds((8 * i + 2 * k + c) * 16, NSEQ)]
                                for kt in range(DT):
                                    ins = e.matmul(out, w[:, kt, c * P:(c + 1) * P], cT[:, kt, :],
                                                   start=(kt == 0), stop=(kt == DT - 1))
                            ins.then_inc(wm_used, 1)
                    e.wait_ge(p_loaded, 16 * 8)
                    e.transpose(PS[:, 4, 0:N_PROW], prow[0:N_PROW, :], ident[0:N_PROW, 0:N_PROW])
                    e.transpose(PS[:, 4, P:P + CONV * CT], crow[0:CONV * CT, :],
                                ident[0:CONV * CT, 0:CONV * CT]).then_inc(p_turned, 1)

                @block.scalar
                def _(e):
                    def load(dst, src):
                        e.dma_start(dst, src).then_inc(p_loaded, 16)
                    load(prow[R_BMOD:R_BMOD + 72, :], A["b_mod"][bass.ds(l, 1)].rearrange("a (r p) -> (a r) p", p=P))
                    load(prow[R_NORM:R_NORM + 24, :],
                         A["norm_w"][bass.ds(l, 1)].rearrange("a k (r p) -> (a k r) p", p=P))
                    load(prow[R_CONVB:R_CONVB + CT, :],
                         A["ssd_conv_b"][bass.ds(l, 1)].rearrange("a (r p) -> (a r) p", p=P))
                    load(prow[R_SNORM:R_SNORM + 3, :],
                         A["ssd_norm_w"][bass.ds(l, 1)].rearrange("a (r p) -> (a r) p", p=P))
                    load(prow[R_BGATE:R_BGATE + 1, :], A["gla_b_gate"][bass.ds(l, 1)])
                    for h in range(2):
                        load(prow[R_GNORM:R_GNORM + 1, h * GV:(h + 1) * GV], A["gla_norm_w"][bass.ds(l, 1)])
                    load(crow[0:CONV * CT, :],
                         A["ssd_conv_w"][bass.ds(l, 1)].rearrange("a k (r p) -> (a k r) p", p=P))

                @block.vector
                def _(e):
                    link = Link(e, "mod_step")
                    e.wait_ge(p_turned, 1)
                    link(e.tensor_copy(cols[:], PS[:, 4, 0:N_PROW]))
                    e.tensor_copy(convw[:], PS[:, 4, P:P + CONV * CT])
                    for b in range(3):
                        n = min(32, 72 - 32 * b)
                        link(e.tensor_tensor(
                            modT[:, 32 * b:32 * b + n, :],
                            PS[:, b, :].rearrange("p (m s) -> p m s", s=16)[:, 0:n, 0:NSEQ],
                            bc(cols[:, R_BMOD + 32 * b:R_BMOD + 32 * b + n], 2, NSEQ), ALU.add))
                    for k in range(3):
                        link(e.scalar_tensor_tensor(
                            out=modA[:, k], in0=modT[:, (3 * k + 1) * DT:(3 * k + 2) * DT, :], scalar=1.0,
                            in1=bc(cols[:, R_NORM + k * DT:R_NORM + (k + 1) * DT], 2, NSEQ),
                            op0=ALU.add, op1=ALU.mult))
                    for m in (2, 8):
                        g = modT[:, m * DT:(m + 1) * DT, :]
                        e.tensor_scalar(g, g, 0.5, None, ALU.mult)

            ffn_block(l, "f1_", 0, 2, U_FF1, U_FO1, U_IN + 2)
            end_stage()

            q = "mx_"
            groups = GROUPS
            NG = len(groups)
            on_act = [g[1] in ("gr", "zx") and g[4] < 3 or n % 2 == 0 for n, g in enumerate(groups)]
            kept_by = [sem("proj_kept_act") if a else sem("proj_kept_dve") for a in on_act]
            kept_no = [sum(1 for m in range(n + 1) if on_act[m] == on_act[n]) for n in range(NG)]
            (ktok,), _ = carve([(NTT, AI)], SCR)
            (cin_rows, cout_rows, tail), _ = carve([(1, CT * P), (2, CT * P), (CT, NB * (CONV - 1))], SCR + NTT * AI)
            cin_rows = cin_rows[:, 0, :]
            NC3 = NB * (CONV - 1)

            with nc.Block(no_gpsimd_drain=True) as block:
                @block.sync
                def _(e):
                    load_units(e, l, U_IN + 2, U_OUT + 2)
                    kv = sem("kv_stored")
                    for t in range(NTT):
                        e.wait_ge(sem("ktok_kept"), t + 1)
                        n = P if t < NCH else TS
                        for name, src in (("k", ktok), ("v", av)):
                            if t < NCH:
                                dst = O[name + "_p"][bass.ds(l, 1), 0, t * P:(t + 1) * P]\
                                    .rearrange("a t h d -> (a t) (h d)")
                            else:
                                dst = O[name + "_s"][bass.ds(l, 1)].rearrange("a b i h d -> (a b i) (h d)")
                            e.dma_start(dst, src[0:n, t, :]).then_inc(kv, 16)
                    e.wait_ge(sem("conv_rows_kept"), 2)
                    e.dma_start(O["conv_p"][bass.ds(l, 1), 0].rearrange("a r n -> (a r) n"),
                                cout_rows[0:CONV - 1, 0, :]).then_inc(kv, 16)
                    e.dma_start(O["conv_s"][bass.ds(l, 1)].rearrange("a b r n -> (a b r) n"),
                                cout_rows[0:NC3, 1, :]).then_inc(kv, 16)
                    e.wait_ge(kv, 16 * (2 * NTT + 2))

                @block.gpsimd
                def _(e):
                    e.memset(U[:, :, 0:CONV - 1], 0.0).then_inc(sem("pads_ready"), 1)
                    e.memset(dtr[:, NCH, :], 0.0).then_inc(sem("pads_ready"), 1)

                @block.tensor
                def _(e):
                    norm_pe(e, q)
                    e.wait_ge(sem("cin_loaded"), 16)
                    for c in range(CT):
                        ins = e.transpose(PS[:, 7, c * NC3:(c + 1) * NC3], cin_rows[0:NC3, c * P:(c + 1) * P],
                                          ident[0:NC3, 0:NC3])
                    ins.then_inc(sem("cin_turned"), 1)
                    e.wait_ge(sem(q + "h_ready"), DT + 1)
                    e.wait_ge(sem("cin_kept"), 1)
                    for n, (u, kind, form, c, m) in enumerate(groups):
                        b = 2 * (n % 4)
                        if n == 0 or groups[n - 1][0] != u:
                            wait_unit(e, U_IN + u)
                        if n >= 4:
                            e.wait_ge(kept_by[n - 4], kept_no[n - 4])
                        width = IN_UNITS[u][2]
                        w = wslot[:, (U_IN + u) % 2, 0:DT * width].rearrange("p (k n) -> p k n", k=DT)
                        for kt in range(DT):
                            if form == "feature":
                                cols_ = w[:, kt, c * P:c * P + (RANK if kind == "lr" else P)]
                                mrows = RANK if kind == "lr" else P
                                for h in range(2):
                                    ins = e.matmul(PS[0:mrows, b + h, 0:HALF], cols_, halves(hT[:, kt, :])[:, h, :],
                                                   start=(kt == 0), stop=(kt == DT - 1))
                            else:
                                nt = P if c < NCH else TS
                                cols_ = w[:, kt, 256:256 + SH] if kind == "dt" else w[:, kt, :]
                                nw = SH if kind == "dt" else width
                                ins = e.matmul(PS[0:nt, b, 0:nw], hT[:, kt, c * P:c * P + nt], cols_,
                                               start=(kt == 0), stop=(kt == DT - 1))
                        ins.then_inc(group_done, 1)
                    for t in range(NTT):
                        nt = P if t < NCH else TS
                        if t == 0:
                            for m in range(NG - 4, NG):
                                e.wait_ge(kept_by[m], kept_no[m])
                        if t >= 2:
                            e.wait_ge(sem("ktok_kept"), t - 1)
                        for j in range(NJ):
                            ins = e.transpose(PS[0:nt, t % 2, j * P:(j + 1) * P], akT[:, j, t * P:t * P + nt], ident[:])
                        ins.then_inc(sem("ktok_turned"), 1)
                    e.wait_ge(sem("tail_ready"), 1)
                    for c in range(CT):
                        e.transpose(PS[0:CONV - 1, 2 + c // 4, (c % 4) * P:(c % 4 + 1) * P],
                                    U[:, c, SEQ:SEQ + CONV - 1], ident[:])
                        ins = e.transpose(PS[0:NC3, 4 + c // 4, (c % 4) * P:(c % 4 + 1) * P],
                                          tail[:, c, :], ident[:])
                    ins.then_inc(sem("conv_rows_turned"), 1)

                def keep(e, n, on_scalar):
                    u, kind, form, c, m = groups[n]
                    b = 2 * (n % 4)
                    e.wait_ge(group_done, U_IN + n + 1)

                    def move(dst, src, f=None, scale=1.0):
                        if on_scalar:
                            return e.activation(dst, src, ACT.Copy if f is None else f, scale=scale)
                        if scale != 1.0:
                            return e.tensor_scalar(dst, src, scale, None, ALU.mult)
                        return e.tensor_copy(dst, src)

                    if kind == "aqk":
                        ins = move(halves((aqT if m < NJ else akT)[:, m % NJ, :]), bank2(b))
                    elif kind == "gqk":
                        if m == 0:
                            ins = move(halves(gqT), bank2(b), scale=GK ** -0.5)
                        else:
                            ins = move(halves(gkT), bank2(b))
                    elif kind == "lr":
                        ins = move(halves(glr[0:RANK, :]), PS[0:RANK, b:b + 2, 0:HALF])
                    elif kind == "gr":
                        ins = move(halves(grT[:, m, :]), bank2(b), ACT.Silu)
                    elif kind in ("av", "gv"):
                        nt = P if c < NCH else TS
                        width = IN_UNITS[u][2]
                        dst = av[0:nt, c, m * width:(m + 1) * width] if kind == "av" else gv[0:nt, c, :]
                        ins = move(dst, PS[0:nt, b, 0:width])
                    elif kind == "dt":
                        nt = P if c < NCH else TS
                        e.wait_ge(sem("pads_ready"), 2)
                        ins = move(dtr[0:nt, c, :], PS[0:nt, b, 0:SH])
                    elif m < 3:
                        ins = move(halves(zT[:, m, :]), bank2(b), ACT.Silu)
                    else:
                        t = m - 3
                        move(U[:, t, CONV - 1:CONV - 1 + HALF], PS[:, b, 0:HALF])
                        move(U[:, t, CONV - 1 + HALF:CONV - 1 + SEQ], PS[:, b + 1, 0:SEQ - HALF])
                        ins = move(Us[:, t, :, CONV - 1:],
                                   PS[:, b + 1, SEQ - HALF:HALF].rearrange("p (b i) -> p b i", i=NI))
                    ins.then_inc(kept_by[n], 1)

                @block.scalar
                def _(e):
                    e.dma_start(cin_rows[0:NC3, :], A["state_ssd_conv"][bass.ds(l, 1)]
                                .rearrange("a b r n -> (a b r) n")).then_inc(sem("cin_loaded"), 16)
                    norm_act(e, q, 1)
                    for n in range(NG):
                        if on_act[n]:
                            keep(e, n, True)
                    e.wait_ge(sem("conv_rows_turned"), 1)
                    for s, r in ((0, CONV - 1), (1, NC3)):
                        e.activation(cout_rows[0:r, s, 0:512], PS[0:r, 2 + 2 * s, :], ACT.Copy)
                        e.activation(cout_rows[0:r, s, 512:CT * P], PS[0:r, 3 + 2 * s, 0:CT * P - 512], ACT.Copy)\
                            .then_inc(sem("conv_rows_kept"), 1)

                @block.vector
                def _(e):
                    e.wait_ge(sem("cin_turned"), 1)
                    e.tensor_copy(Us[:, :, :, 0:CONV - 1],
                                  PS[:, 7, 0:CT * NC3].rearrange("p (c b r) -> p c b r", c=CT, b=NB))\
                        .then_inc(sem("cin_kept"), 1)
                    norm_dve(e, q, 1)
                    for n in range(NG):
                        if not on_act[n]:
                            keep(e, n, False)
                    e.wait_ge(sem("proj_kept_act"), sum(on_act))
                    e.wait_ge(sem("proj_kept_dve"), NG - sum(on_act))
                    e.tensor_copy(tail.rearrange("p c (b r) -> p c b r", b=NB), Us[:, :, :, NI:NI + CONV - 1])\
                        .then_inc(sem("tail_ready"), 1)
                    for t in range(NTT):
                        nt = P if t < NCH else TS
                        e.wait_ge(sem("ktok_turned"), t + 1)
                        e.tensor_copy(ktok[0:nt, t, :], PS[0:nt, t % 2, 0:AI]).then_inc(sem("ktok_kept"), 1)

            NU = AH * NCH
            (vc, kc, qbd, KT), at = carve([(NB, 2, AI), (2, 2, AI), (NJ, NB * 144), (2, NJ, PAST)], SCR)
            (Sn, Pr, PT), _ = carve([(2, SEQ), (2, SEQ), (2, NCH, P)], at)
            (Snd, Pd, PTd), _ = carve([(NJ, PAST + TS), (NJ, PAST + TS), (NJ, 3 * P)], at)
            scale = AD ** -0.5
            nmax, rsum = small[:, 0:NU], small[:, NU:2 * NU]
            nmaxd, rsumd = small[:, 2 * NU:2 * NU + NJ], small[:, 2 * NU + NJ:2 * NU + 2 * NJ]
            k_loaded = [sem("k_loaded0"), sem("k_loaded1")]
            with nc.Block(no_gpsimd_drain=True) as block:
                @block.sync
                def _(e):
                    def cache(name, b):
                        return A[name][bass.ds(l, 1), b].rearrange("a (s p) h d -> p (a s) (h d)", p=P)
                    for b in range(NB):
                        if b >= 2:
                            e.wait_ge(sem("k_turned"), b - 1)
                        e.dma_start(kc[:, b % 2], cache("cache_attn_k", b)).then_inc(k_loaded[b % 2], 16)
                        if b < 2:
                            for c in range(4 * b, 4 * b + 4):
                                e.dma_start(vc[:, c], cache("cache_attn_v", c)).then_inc(sem("v_loaded"), 16)

                @block.gpsimd
                def _(e):
                    e.memset(qbd[:], 0.0).then_inc(sem("qbd_zero"), 1)

                @block.tensor
                def _(e):
                    def scores(u):
                        h, i = divmod(u, NCH)
                        r = slice((h % 2) * AD, (h % 2 + 1) * AD)
                        if u >= 2:
                            e.wait_ge(sem("neg_scores"), u - 1)
                        e.matmul(PS[:, u % 2, 0:(i + 1) * P], aqT[r, h // 2, i * P:(i + 1) * P],
                                 akT[r, h // 2, 0:(i + 1) * P], start=True, stop=True).then_inc(sem("scored"), 1)

                    def turn(u):
                        i = u % NCH
                        e.wait_ge(sem("p_ready"), u + 1)
                        if u >= 2:
                            e.wait_ge(sem("pt_kept"), u - 1)
                        for s in range(i + 1):
                            ins = e.transpose(PS[:, 2 + u % 2, s * P:(s + 1) * P], Pr[:, u % 2, s * P:(s + 1) * P],
                                              ident[:])
                        ins.then_inc(sem("pt_turned"), 1)

                    def values(u):
                        h, i = divmod(u, NCH)
                        r = slice((h % 2) * AD, (h % 2 + 1) * AD)
                        e.wait_ge(sem("pt_kept"), u + 1)
                        if u >= 2:
                            e.wait_ge(sem("o_kept"), u - 1)
                        for s in range(i + 1):
                            ins = e.matmul(PS[r, 4 + u % 2, 0:P], av[:, s, h * AD:(h + 1) * AD], PT[:, u % 2, s, :],
                                           start=(s == 0), stop=(s == i))
                        ins.then_inc(sem("o_done"), 1)

                    for s in range(NU + 2):
                        if s < NU:
                            scores(s)
                        if 1 <= s <= NU:
                            turn(s - 1)
                        if s >= 2:
                            values(s - 2)

                    e.wait_ge(sem("qbd_ready"), 2 * NJ)
                    e.wait_ge(sem("pt_kept"), NU)
                    for b in range(NB):
                        e.wait_ge(k_loaded[b % 2], 16 * (b // 2 + 1))
                        if b >= 1:
                            e.wait_ge(sem("kT_kept"), b)
                        for j in range(NJ):
                            for s in range(2):
                                ins = e.transpose(PS[:, 6 + j // 2, (j % 2) * PAST + s * P:(j % 2) * PAST + (s + 1) * P],
                                                  kc[:, b % 2, s, j * P:(j + 1) * P], ident[:])
                        ins.then_inc(sem("k_turned"), 1)
                        e.wait_ge(sem("kT_kept"), b + 1)
                        for j in range(NJ):
                            ins = e.matmul(PS[:, j, 0:PAST], qbd[:, j, b * P:(b + 1) * P], KT[:, b % 2, j, :],
                                           start=(b == 0), stop=False, skip_group_check=True)
                        ins.then_inc(sem("k_used"), 1)
                        for j in range(NJ):
                            ins = e.matmul(PS[:, j, PAST:PAST + TS], qbd[:, j, b * P:(b + 1) * P], akT[:, j, SEQ:T],
                                           start=False, stop=(b == NB - 1), skip_group_check=True)
                    ins.then_inc(sem("dec_scored"), 1)
                    e.wait_ge(sem("o_kept"), NU)
                    for j in range(NJ):
                        e.wait_ge(sem("dec_p_ready"), j + 1)
                        e.transpose(PS[:, 3 + j, 0:P], Pd[:, j, 0:P], ident[:])
                        e.transpose(PS[:, 3 + j, P:2 * P], Pd[:, j, P:2 * P], ident[:])
                        e.transpose(PS[0:TS, 3 + j, 2 * P:3 * P], Pd[:, j, PAST:PAST + TS], ident[:])\
                            .then_inc(sem("dec_pt_turned"), 1)
                    e.wait_ge(sem("v_loaded"), 16 * NB)
                    for j in range(NJ):
                        e.wait_ge(sem("dec_pt_kept"), j + 1)
                        out = PS[:, j, 384:512]
                        e.matmul(out, av[0:TS, NCH, j * P:(j + 1) * P], PTd[0:TS, j, 2 * P:3 * P],
                                 start=True, stop=False, skip_group_check=True)
                        for b in range(NB):
                            for s in range(2):
                                ins = e.matmul(out[:, b * 16:(b + 1) * 16], vc[:, b, s, j * P:(j + 1) * P],
                                               PTd[:, j, s * P + b * 16:s * P + (b + 1) * 16], start=False,
                                               stop=(b == NB - 1 and s == 1), skip_group_check=True)
                        ins.then_inc(sem("dec_o_done"), 1)

                @block.scalar
                def _(e):
                    e.preload_act_table(ACT.Exp)

                    def exps(u):
                        w = (u % NCH + 1) * P
                        e.wait_ge(sem("neg_max"), u + 1)
                        if u >= 2:
                            e.wait_ge(sem("pt_turned"), u - 1)
                        e.activation(Pr[:, u % 2, 0:w], Sn[:, u % 2, 0:w], ACT.Exp, scale=-1.0, bias=nmax[:, u:u + 1],
                                     accum_out=rsum[:, u:u + 1]).then_inc(sem("exps_done"), 1)

                    def o_copy(u):
                        h, i = divmod(u, NCH)
                        r = slice((h % 2) * AD, (h % 2 + 1) * AD)
                        e.wait_ge(sem("o_done"), u + 1)
                        e.activation(hT[r, 5 + h // 2, i * P:(i + 1) * P], PS[r, 4 + u % 2, 0:P], ACT.Copy)\
                            .then_inc(sem("o_kept"), 1)

                    for s in range(NU + 2):
                        if s < NU:
                            exps(s)
                        if s >= 2:
                            o_copy(s - 2)
                    for b in range(NB):
                        e.wait_ge(sem("k_turned"), b + 1)
                        if b >= 2:
                            e.wait_ge(sem("k_used"), b - 1)
                        e.activation(KT[:, b % 2, 0:2, :], PS[:, 6, :].rearrange("p (j s) -> p j s", j=2), ACT.Copy)
                        e.activation(KT[:, b % 2, 2, :], PS[:, 7, 0:PAST], ACT.Copy).then_inc(sem("kT_kept"), 1)
                    for j in range(NJ):
                        e.wait_ge(sem("dec_neg_max"), j + 1)
                        e.activation(Pd[:, j, :], Snd[:, j, :], ACT.Exp, scale=-1.0, bias=nmaxd[:, j:j + 1],
                                     accum_out=rsumd[:, j:j + 1]).then_inc(sem("dec_exps"), 1)
                    for j in range(NJ):
                        e.wait_ge(sem("dec_o_done"), j + 1)
                        for h2 in range(2):
                            r = slice(h2 * AD, (h2 + 1) * AD)
                            e.activation(hT[r, 5 + j, SEQ:T].rearrange("p (b i) -> p b i", i=NI),
                                         PS[r, j, 384:512].rearrange("p (b i) -> p b i", i=16)[:, :, h2 * NI:(h2 + 1) * NI],
                                         ACT.Copy)

                @block.vector
                def _(e):
                    link = Link(e, "att_step")

                    def negate(u):
                        i = u % NCH
                        w = (i + 1) * P
                        e.wait_ge(sem("scored"), u + 1)
                        if u >= 2:
                            e.wait_ge(sem("exps_done"), u - 1)
                        e.scalar_tensor_tensor(out=Sn[:, u % 2, 0:w], in0=PS[:, u % 2, 0:w], scalar=-scale,
                                               in1=nwin[:, SEQ - w:SEQ], op0=ALU.mult, op1=ALU.add)\
                            .then_inc(sem("neg_scores"), 1)
                        e.wait_ge(sem("neg_scores"), u + 1)
                        e.tensor_reduce(nmax[:, u:u + 1], Sn[:, u % 2, 0:w], AX.X, ALU.min).then_inc(sem("neg_max"), 1)

                    def normalize(u):
                        w = (u % NCH + 1) * P
                        e.wait_ge(sem("exps_done"), u + 1)
                        link(e.reciprocal(rsum[:, u:u + 1], rsum[:, u:u + 1]))
                        e.tensor_scalar(Pr[:, u % 2, 0:w], Pr[:, u % 2, 0:w], rsum[:, u:u + 1], None, ALU.mult)\
                            .then_inc(sem("p_ready"), 1)

                    def keep_pt(u):
                        i = u % NCH
                        e.wait_ge(sem("pt_turned"), u + 1)
                        if u >= 2:
                            e.wait_ge(sem("o_done"), u - 1)
                        e.tensor_copy(PT[:, u % 2, 0:i + 1, :],
                                      PS[:, 2 + u % 2, 0:(i + 1) * P].rearrange("p (s t) -> p s t", t=P))\
                            .then_inc(sem("pt_kept"), 1)

                    e.wait_ge(sem("qbd_zero"), 1)
                    for j in range(NJ):
                        for h2 in range(2):
                            r = slice(h2 * AD, (h2 + 1) * AD)
                            e.tensor_copy(qbd[r, j, :].rearrange("p (b i) -> p b i", i=144)[:, :, h2 * NI:(h2 + 1) * NI],
                                          aqT[r, j, SEQ:T].rearrange("p (b i) -> p b i", i=NI))\
                                .then_inc(sem("qbd_ready"), 1)
                    for s in range(NU + 1):
                        if s < NU:
                            negate(s)
                        if s >= 1:
                            normalize(s - 1)
                            keep_pt(s - 1)
                    e.wait_ge(sem("dec_scored"), 1)
                    e.wait_ge(sem("o_done"), NU)
                    for j in range(NJ):
                        e.scalar_tensor_tensor(out=Snd[:, j, :], in0=PS[:, j, 0:PAST + TS], scalar=-scale, in1=ndec[:],
                                               op0=ALU.mult, op1=ALU.add).then_inc(sem("dec_neg"), 1)
                    for j in range(NJ):
                        e.wait_ge(sem("dec_neg"), j + 1)
                        e.tensor_reduce(nmaxd[:, j:j + 1], Snd[:, j, :], AX.X, ALU.min).then_inc(sem("dec_neg_max"), 1)
                    for j in range(NJ):
                        e.wait_ge(sem("dec_exps"), j + 1)
                        link(e.reciprocal(rsumd[:, j:j + 1], rsumd[:, j:j + 1]))
                        e.tensor_scalar(Pd[:, j, :], Pd[:, j, :], rsumd[:, j:j + 1], None, ALU.mult)\
                            .then_inc(sem("dec_p_ready"), 1)
                    for j in range(NJ):
                        e.wait_ge(sem("dec_pt_turned"), j + 1)
                        e.tensor_copy(PTd[:, j, 0:PAST], PS[:, 3 + j, 0:PAST])
                        e.tensor_copy(PTd[0:TS, j, PAST:PAST + P], PS[0:TS, 3 + j, PAST:PAST + P])\
                            .then_inc(sem("dec_pt_kept"), 1)

            end_stage()

            LEVELS = [None, 6, 5, 4, 3, 2, 1, 0]
            (G, ga, gb, X, qx, kx, eG, qE, kE, W, Ws, kEt, St, S0, kEm, Sn_, oT, wg), _ = carve(
                [(1, T), (1, T), (1, T), (2, T), (2, T), (2, T), (1, T), (1, T), (1, T), (GH, SEQ), (GH, TS),
                 (NTT, P), (2, GDV), (NB, GDV), (NB, P), (NB, GDV), (2, T), (1, P)], ATT_IN)
            G, ga, gb, eG, qE, kE, wg = [v[:, 0, :] for v in (G, ga, gb, eG, qE, kE, wg)]
            with nc.Block(no_gpsimd_drain=True) as block:
                @block.sync
                def _(e):
                    e.dma_start(wg[0:RANK, :], A["gla_w_gate"][bass.ds(l, 1)].rearrange("a r k -> (a r) k"))\
                        .then_inc(sem("wg_loaded"), 16)
                    e.wait_ge(sem("gla_zero"), 2)
                    for h in range(GH):
                        e.dma_start(S0[h * GK:(h + 1) * GK, :, h * GV:(h + 1) * GV],
                                    A["state_gla"][bass.ds(l, 1), :, h].rearrange("a b k v -> k (a b) v"))\
                            .then_inc(sem("s0_loaded"), 16)
                    e.wait_ge(sem("gla_state"), 2 * NCH)
                    for h in range(GH):
                        e.dma_start(O["gla_p"][bass.ds(l, 1), 0, h].rearrange("a k v -> (a k) v"),
                                    St[h * GK:(h + 1) * GK, NCH % 2, h * GV:(h + 1) * GV]).then_inc(sem("gla_stored"), 16)
                    e.wait_ge(sem("gla_new"), 2)
                    for h in range(GH):
                        e.dma_start(O["gla_s"][bass.ds(l, 1), :, h].rearrange("a b k v -> k (a b) v"),
                                    Sn_[h * GK:(h + 1) * GK, :, h * GV:(h + 1) * GV]).then_inc(sem("gla_stored"), 16)
                    e.wait_ge(sem("gla_stored"), 16 * 2 * GH)

                @block.gpsimd
                def _(e):
                    e.memset(S0[:], 0.0).then_inc(sem("gla_zero"), 1)
                    e.memset(St[:, 0, :], 0.0).then_inc(sem("gla_zero"), 1)

                @block.tensor
                def _(e):
                    e.wait_ge(sem("wg_loaded"), 16)
                    for h in range(2):
                        ins = e.matmul(PS[:, h, 0:HALF], wg[0:RANK, :], halves(glr[0:RANK, :])[:, h, :],
                                       start=True, stop=True)
                    ins.then_inc(sem("gate_in"), 1)
                    for n, k in enumerate(LEVELS):
                        q_, k_ = (gqT, gkT) if n == 0 else (qx[:, n % 2, :], kx[:, n % 2, :])
                        if n == 0:
                            e.wait_ge(sem("gate_biased"), 1)
                        else:
                            e.wait_ge(sem("lev_qk"), 2 * n)
                            e.wait_ge(sem("lev_kept"), n)
                        for h in range(GH):
                            r = slice(h * GK, (h + 1) * GK)
                            for c in range(NCH):
                                ins = e.matmul(PS[:, h, c * P:(c + 1) * P], k_[r, c * P:(c + 1) * P],
                                               q_[r, c * P:(c + 1) * P], start=True, stop=True,
                                               tile_position=(h * GK, 0))
                            if n == 0 or k <= 2:
                                ins = e.matmul(PS[0:TS, 4 + h, 0:TS], k_[r, SEQ:T], q_[r, SEQ:T], start=True,
                                               stop=True, tile_position=(h * GK, 0))
                        ins.then_inc(sem("lev_scored"), 1)
                    e.wait_ge(sem("lev_kept"), len(LEVELS))
                    e.wait_ge(sem("kE_ready"), 2)
                    for c in range(NCH):
                        e.transpose(PS[:, 4, c * P:(c + 1) * P], kE[:, c * P:(c + 1) * P], ident[:])
                    e.transpose(PS[0:TS, 5, 0:P], kE[:, SEQ:T], ident[:]).then_inc(sem("kE_turned"), 1)
                    e.wait_ge(sem("kEt_kept"), 2)
                    e.wait_ge(sem("gla_zero"), 2)

                    def intra(out, rows, tt, w, h):
                        return e.matmul(out, gv[rows, tt, h * GV:(h + 1) * GV], w, start=False, stop=True,
                                        skip_group_check=True)

                    for c in range(NCH):
                        if c >= 2:
                            e.wait_ge(sem("gla_masked"), c - 1)
                        e.matmul(PS[:, 6 + c % 2, 0:GDV], kEt[:, c, :], gv[:, c, :], start=True, stop=True)\
                            .then_inc(sem("gla_local"), 1)
                        if c >= 1:
                            e.wait_ge(sem("gla_state"), 2 * c)
                        for p2 in range(2):
                            e.matmul(PS[:, p2, c * P:(c + 1) * P], St[:, c % 2, p2 * P:(p2 + 1) * P],
                                     qE[:, c * P:(c + 1) * P], start=True, stop=False, skip_group_check=True)
                            for h2 in range(2):
                                h = 2 * p2 + h2
                                ins = intra(PS[h2 * GV:(h2 + 1) * GV, p2, c * P:(c + 1) * P], slice(0, P), c,
                                            W[:, h, c * P:(c + 1) * P], h)
                        ins.then_inc(sem("gla_o"), 1)
                    e.wait_ge(sem("s0_loaded"), 16 * GH)
                    for p2 in range(2):
                        for b in range(NB):
                            e.matmul(PS[:, 2, p2 * TS + b * NI:p2 * TS + (b + 1) * NI], S0[:, b, p2 * P:(p2 + 1) * P],
                                     qE[:, SEQ + b * NI:SEQ + (b + 1) * NI], start=(p2 == 0 and b == 0), stop=False,
                                     skip_group_check=True)
                    for h in range(GH):
                        p2, h2 = divmod(h, 2)
                        ins = intra(PS[h2 * GV:(h2 + 1) * GV, 2, p2 * TS:(p2 + 1) * TS], slice(0, TS), NCH,
                                    Ws[0:TS, h, :], h)
                    ins.then_inc(sem("gla_o"), 1)
                    e.wait_ge(sem("kEm_ready"), 1)
                    e.wait_ge(sem("gla_masked"), NCH)
                    for b in range(NB):
                        ins = e.matmul(PS[:, 4 + b // 2, (b % 2) * GDV:(b % 2 + 1) * GDV], kEm[0:TS, b, :],
                                       gv[0:TS, NCH, :], start=True, stop=True)
                    ins.then_inc(sem("gla_new_local"), 1)
                    e.wait_ge(sem("o_squares"), 2)
                    for p2 in range(2):
                        for h in range(2):
                            ins = e.matmul(PS[:, 2 * p2 + h, 0:HALF], bd64[:], halves(qx[:, p2, :])[:, h, :],
                                           start=True, stop=True)
                    ins.then_inc(sem("o_sumsq"), 1)

                @block.scalar
                def _(e):
                    e.wait_ge(sem("gate_abs"), 1)
                    e.activation(ga, ga, ACT.Exp, scale=-1.0).then_inc(sem("gate_exp"), 1)
                    e.wait_ge(sem("gate_exp"), 1)
                    e.activation(ga, ga, ACT.Ln, bias=ones[:, 0:1]).then_inc(sem("gate_ln"), 1)
                    e.wait_ge(sem("g_sum"), 1)
                    e.activation(eG, G, ACT.Exp).then_inc(sem("eG_ready"), 1)
                    e.wait_ge(sem("g_end"), 2)
                    e.activation(kE, gb, ACT.Exp, scale=-1.0).then_inc(sem("kE_exp"), 1)
                    for n in range(1, len(LEVELS)):
                        w = SEQ if LEVELS[n] > 2 else T
                        e.wait_ge(sem("lev_abs"), n)
                        e.activation(X[:, n % 2, 0:w], X[:, n % 2, 0:w], ACT.Exp, scale=-1.0).then_inc(sem("lev_exp"), 1)
                    e.wait_ge(sem("kE_turned"), 1)
                    e.activation(kEt[:, 0:NCH, :], PS[:, 4, :].rearrange("p (c k) -> p c k", k=P), ACT.Copy)\
                        .then_inc(sem("kEt_kept"), 1)
                    e.activation(kEt[0:TS, NCH, :], PS[0:TS, 5, 0:P], ACT.Copy).then_inc(sem("kEt_kept"), 1)
                    e.wait_ge(sem("gla_o"), NCH + 1)
                    e.activation(oT[:, :, 0:SEQ], PS[:, 0:2, :], ACT.Copy).then_inc(sem("oT_kept"), 1)
                    e.activation(oT[:, :, SEQ:T], PS[:, 2, 0:2 * TS].rearrange("p (a t) -> p a t", a=2), ACT.Copy)\
                        .then_inc(sem("oT_kept"), 1)
                    e.wait_ge(sem("oT_kept"), 2)
                    e.wait_ge(sem("lev_scored"), len(LEVELS))
                    for p2 in range(2):
                        e.activation(qx[:, p2, :], oT[:, p2, :], ACT.Square).then_inc(sem("o_squares"), 1)
                    e.wait_ge(sem("o_sumsq"), 1)
                    for p2 in range(2):
                        e.activation(halves(kx[:, p2, :]), bank2(2 * p2), ACT.Sqrt, scale=1.0 / GV, bias=epsc[:])\
                            .then_inc(sem("o_root"), 1)

                @block.vector
                def _(e):
                    link = Link(e, "gla_step")
                    e.wait_ge(sem("gate_in"), 1)
                    e.tensor_scalar(halves(G), bank2(0), cols[:, R_BGATE:R_BGATE + 1], None, ALU.add)\
                        .then_inc(sem("gate_biased"), 1)
                    e.wait_ge(sem("gate_biased"), 1)
                    absolute(e, ga, G).then_inc(sem("gate_abs"), 1)
                    link(e.tensor_scalar(gb, G, 0.0, None, ALU.min))
                    e.wait_ge(sem("gate_ln"), 1)
                    link(e.tensor_tensor(gb, gb, ga, ALU.subtract))
                    link(e.tensor_scalar(gb, gb, 1.0 / TAU, None, ALU.mult))
                    e.tensor_tensor_scan(G, rmask[:], gb, 0.0, ALU.mult, ALU.add).then_inc(sem("g_sum"), 1)
                    e.wait_ge(sem("g_sum"), 1)
                    for a, z, w in ((0, SEQ, P), (SEQ, T, NI)):
                        g3 = G[:, a:z].rearrange("p (c t) -> p c t", t=w)
                        e.tensor_tensor(gb[:, a:z].rearrange("p (c t) -> p c t", t=w), g3,
                                        g3[:, :, w - 1:w].to_broadcast([P, (z - a) // w, w]), ALU.subtract)\
                            .then_inc(sem("g_end"), 1)

                    def exponent(n):
                        k = LEVELS[n]
                        w, span = (SEQ if k > 2 else T), 2 ** (k + 1)
                        g3 = G[:, 0:w].rearrange("p (c t) -> p c t", t=span)
                        if n >= 3:
                            e.wait_ge(sem("lev_qk"), 2 * (n - 2))
                        link(e.tensor_tensor(X[:, n % 2, 0:w].rearrange("p (c t) -> p c t", t=span), g3,
                                             g3[:, :, span // 2 - 1:span // 2].to_broadcast([P, w // span, span]),
                                             ALU.subtract))
                        absolute(e, X[:, n % 2, 0:w], X[:, n % 2, 0:w])\
                            .then_inc(sem("lev_abs"), 1)

                    def scaled(n):
                        w = SEQ if LEVELS[n] > 2 else T
                        e.wait_ge(sem("lev_exp"), n)
                        if n >= 3:
                            e.wait_ge(sem("lev_scored"), n - 1)
                        for dst, src in ((qx, gqT), (kx, gkT)):
                            e.tensor_tensor(dst[:, n % 2, 0:w], src[:, 0:w], X[:, n % 2, 0:w], ALU.mult)\
                                .then_inc(sem("lev_qk"), 1)

                    def keep(n):
                        m = 0 if n == 0 else 1 + LEVELS[n]
                        e.wait_ge(sem("lev_scored"), n + 1)
                        w4 = W.rearrange("p h (c t) -> p h c t", t=P)
                        p4 = PS[:, 0:GH, :].rearrange("p h (c t) -> p h c t", t=P)
                        m4 = bc(bc(levm[:, m, :], 1, NCH), 1, GH)
                        ws, ps, ms = Ws[0:TS], PS[0:TS, 4:4 + GH, 0:TS], bc(levm[0:TS, m, 0:TS], 1, GH)
                        if n == 0:
                            link(e.tensor_tensor(ws, ps, ms, ALU.mult))
                            ins = e.tensor_tensor(w4, p4, m4, ALU.mult)
                        else:
                            if LEVELS[n] <= 2:
                                link(e.copy_predicated(ws, ms.bitcast(I32), ps))
                            ins = e.copy_predicated(w4, m4.bitcast(I32), p4)
                        ins.then_inc(sem("lev_kept"), 1)
                        e.wait_ge(sem("lev_kept"), n + 1)

                    for n in range(len(LEVELS)):
                        if n + 1 < len(LEVELS):
                            exponent(n + 1)
                        keep(n)
                        if n + 1 < len(LEVELS):
                            scaled(n + 1)
                        if n == 0:
                            e.wait_ge(sem("kE_exp"), 1)
                            e.tensor_tensor(kE, kE, gkT, ALU.mult).then_inc(sem("kE_ready"), 1)
                            e.tensor_tensor(qE, eG, gqT, ALU.mult).then_inc(sem("kE_ready"), 1)
                    e.wait_ge(sem("kEt_kept"), 2)
                    e.tensor_tensor(kEm[0:TS], bc(kEt[0:TS, NCH, :], 1, NB), bc(bsel[:], 2, P), ALU.mult)\
                        .then_inc(sem("kEm_ready"), 1)
                    e.wait_ge(sem("gla_zero"), 2)
                    masked = ga[:, 0:GDV]
                    for c in range(NCH):
                        e.wait_ge(sem("gla_local"), c + 1)
                        e.tensor_tensor(masked, PS[:, 6 + c % 2, 0:GDV], hmask[:], ALU.mult)\
                            .then_inc(sem("gla_masked"), 1)
                        if c >= 1:
                            e.wait_ge(sem("gla_o"), c)
                        e.tensor_scalar(St[:, (c + 1) % 2, :], St[:, c % 2, :], eG[:, (c + 1) * P - 1:(c + 1) * P], None,
                                        ALU.mult).then_inc(sem("gla_state"), 1)
                        e.wait_ge(sem("gla_masked"), c + 1)
                        e.wait_ge(sem("gla_state"), 2 * c + 1)
                        e.tensor_tensor(St[:, (c + 1) % 2, :], St[:, (c + 1) % 2, :], masked, ALU.add)\
                            .then_inc(sem("gla_state"), 1)
                        e.wait_ge(sem("gla_state"), 2 * c + 2)
                    e.wait_ge(sem("s0_loaded"), 16 * GH)
                    e.tensor_tensor(Sn_[:], S0[:], bc(eG[:, SEQ + NI - 1:T:NI], 2, GDV), ALU.mult)\
                        .then_inc(sem("gla_new"), 1)
                    e.wait_ge(sem("gla_new"), 1)
                    e.wait_ge(sem("gla_new_local"), 1)
                    flat = Sn_.rearrange("p b v -> p (b v)")
                    e.tensor_tensor(flat, PS[:, 4:8, :].rearrange("p b n -> p (b n)"), flat, ALU.add)\
                        .then_inc(sem("gla_new"), 1)
                    e.wait_ge(sem("o_root"), 2)
                    link(e.reciprocal(kx[:], kx[:]))
                    link(e.tensor_tensor(oT[:], oT[:], kx[:], ALU.mult))
                    for p2 in range(2):
                        e.scalar_tensor_tensor(out=hT[:, 3 + p2, :], in0=oT[:, p2, :], scalar=cols[:, R_GNORM:R_GNORM + 1],
                                               in1=grT[:, p2, :], op0=ALU.mult, op1=ALU.mult)

            end_stage()

            (xc, xt, Bt, xdt, Gm, E_, EC, cbm, Wt, CE, xdE, ST, h0n, Btm, sN, aexp, stT, tiny), at = carve(
                [(CT, T), (NTT, SI), (NTT, SG * SN), (NTT, SI), (2, SH * P), (SH, P), (SH, P), (SG, P), (SH, P),
                 (SH, P), (1, SI), (2, SI), (NB, NJ, P), (NB, SG * SN), (NB, NJ, P), (SH, SP_), (NJ, P), (14, 32)],
                SSD_SCR)
            (h0T,), _ = carve([(NB, SI)], 3 * T)
            xdE = xdE[:, 0, :]
            (dt_x, dt_abs, dt_pos, dt_one, dt_ln, dt_eq, dt_, a_) = [tiny[:, i, 0:NTT * SH] for i in range(8)]
            bias6, alog6, dcol, te = tiny[:, 8, 0:SH], tiny[:, 9, 0:SH], tiny[:, 10, 0:NJ], tiny[:, 11, 0:SH]
            decN, d6 = tiny[:, 12, 0:NJ * NB], tiny[:, 13, 0:SH]
            R3 = SH // SG

            def tok(c):
                return (slice(c * P, (c + 1) * P), P) if c < NCH else (slice(SEQ, T), TS)

            with nc.Block(no_gpsimd_drain=True) as block:
                @block.sync
                def _(e):
                    def small_load(dst, src):
                        e.dma_start(dst, src).then_inc(sem("ssd_params"), 16)
                    small_load(bias6, A["ssd_dt_bias"][bass.ds(l, 1)].to_broadcast([P, SH]))
                    small_load(alog6, A["ssd_a_log"][bass.ds(l, 1)].to_broadcast([P, SH]))
                    small_load(d6, A["ssd_d"][bass.ds(l, 1)].to_broadcast([P, SH]))
                    for b in range(NB):
                        e.dma_start(h0n[:, b], A["state_ssd"][bass.ds(l, 1), b]
                                    .rearrange("a (j t) p n -> (t p) (a j) n", t=2)).then_inc(sem("h0_loaded"), 16)
                    e.wait_ge(sem("stT_kept"), 1)
                    e.dma_start(O["ssd_p"][bass.ds(l, 1), 0].rearrange("a (j t) p n -> (t p) (a j) n", t=2), stT[:])\
                        .then_inc(sem("ssd_stored"), 16)
                    e.wait_ge(sem("ssd_new"), 2)
                    for b in range(NB):
                        e.dma_start(O["ssd_s"][bass.ds(l, 1), b].rearrange("a (j t) p n -> (t p) (a j) n", t=2),
                                    sN[:, b]).then_inc(sem("ssd_stored"), 16)
                    e.wait_ge(sem("ssd_stored"), 16 * (NB + 1))

                @block.gpsimd
                def _(e):
                    e.memset(ST[:, 0, :], 0.0).then_inc(sem("ssd_zero"), 1)

                @block.tensor
                def _(e):
                    for c in range(NTT):
                        s, n = tok(c)
                        if c == 0:
                            e.wait_ge(sem("conv_silu"), CT)
                        if c >= 2:
                            e.wait_ge(sem("xt_kept"), c - 1)
                            e.wait_ge(sem("Bt_kept"), c - 1)
                        for t in range(5):
                            o = PS[0:n, 2 * (c % 2), t * P:(t + 1) * P] if t < 3 else \
                                PS[0:n, 2 * (c % 2) + 1, (t - 3) * P:(t - 2) * P]
                            ins = e.transpose(o, xc[:, t, s], ident[:])
                        ins.then_inc(sem("xt_turned"), 1)
                    e.wait_ge(sem("h0_loaded"), 16 * NB)
                    for b in range(NB):
                        if b >= 2:
                            e.wait_ge(sem("h0T_kept"), b - 1)
                        for j in range(NJ):
                            ins = e.transpose(PS[:, 6 + b % 2, j * P:(j + 1) * P], h0n[:, b, j, :], ident[:])
                        ins.then_inc(sem("h0_turned"), 1)
                    e.wait_ge(sem("xt_kept"), NTT)
                    e.wait_ge(sem("Bt_kept"), NTT)
                    e.wait_ge(sem("h0T_kept"), NB)

                    def segments(c):
                        s, n = tok(c)
                        gt = gts[:] if c < NCH else gt8[:]
                        g3 = Gm[:, c % 2, :].rearrange("p (h t) -> p h t", t=P)
                        e.wait_ge(sem("gm_ready"), c + 1)
                        if c >= 1:
                            e.wait_ge(sem("ssd_exps"), c)
                            e.wait_ge(sem("cbm_ready"), c)
                        for i, (a, z) in enumerate(((0, 4), (4, SH))):
                            e.matmul(PS[0:n, i, 0:(z - a) * n], gt, g3[0:n, a:z, 0:n], start=True, stop=True)
                            e.matmul(PS[:, 2 + i, 0:(z - a) * n], ones[0:n, :], g3[0:n, a:z, 0:n], start=True, stop=True)
                        if c == NCH:
                            e.matmul(PS[0:n, 7, 0:SH], gt, a_[0:n, NCH * SH:NTT * SH], start=True, stop=True)
                        for g in range(SG):
                            ins = e.matmul(PS[0:n, 4, g * n:(g + 1) * n], xc[:, 3 + g, s], xc[:, 5 + g, s],
                                           start=True, stop=True)
                        ins.then_inc(sem("seg_done"), 1)

                    def outputs(c):
                        s, n = tok(c)
                        e.wait_ge(sem("ssd_parts"), 3 * c + 3)
                        if c >= 1:
                            e.wait_ge(sem("y_kept"), NJ * c)
                        if 1 <= c < NCH:
                            e.wait_ge(sem("ssd_state"), 2 * c)
                        for h in range(SH):
                            j, h2 = divmod(h, 2)
                            o = PS[h2 * 64:(h2 + 1) * 64, 5, j * n:(j + 1) * n]
                            e.matmul(o, xdt[0:n, c, h * SP_:(h + 1) * SP_], Wt[0:n, h, 0:n], start=True, stop=False,
                                     skip_group_check=True)
                            if c < NCH:
                                ins = e.matmul(o, ST[:, c % 2, h * SP_:(h + 1) * SP_], CE[:, h, :], start=False,
                                               stop=True, skip_group_check=True)
                                continue
                            for b in range(NB):
                                ins = e.matmul(o[:, b * NI:(b + 1) * NI], h0T[:, b, h * SP_:(h + 1) * SP_],
                                               CE[:, h, b * NI:(b + 1) * NI], start=False, stop=(b == NB - 1),
                                               skip_group_check=True)
                        ins.then_inc(sem("y_done"), 1)
                        if c < NCH:
                            if c >= 1:
                                e.wait_ge(sem("ssd_state"), 2 * c)
                            for g in range(SG):
                                ins = e.matmul(PS[:, 6, g * R3 * SP_:(g + 1) * R3 * SP_], Bt[:, c, g * SN:(g + 1) * SN],
                                               xdE[:, g * R3 * SP_:(g + 1) * R3 * SP_], start=True, stop=True)
                            ins.then_inc(sem("ssd_local"), 1)

                    segments(0)
                    for c in range(NTT):
                        if c + 1 < NTT:
                            segments(c + 1)
                        outputs(c)
                    e.wait_ge(sem("ssd_state"), 2 * NCH)
                    for j in range(NJ):
                        ins = e.transpose(PS[:, 7, j * P:(j + 1) * P], ST[:, NCH % 2, j * P:(j + 1) * P], ident[:])
                    ins.then_inc(sem("st_turned"), 1)
                    e.wait_ge(sem("aexp_ready"), 1)
                    for j in range(NJ):
                        ins = e.matmul(PS[:, 7, 3 * P + j * NB:3 * P + (j + 1) * NB],
                                       aexp[0:TS, 2 * j:2 * j + 2, :].rearrange("p a b -> p (a b)"), bsel[:],
                                       start=True, stop=True)
                    ins.then_inc(sem("decn_done"), 1)
                    e.wait_ge(sem("y_kept"), NJ * NTT)
                    e.wait_ge(sem("Btm_ready"), 1)
                    for b in range(NB):
                        for h in range(SH):
                            j, h2 = divmod(h, 2)
                            m = b * NJ + j
                            ins = e.matmul(PS[h2 * 64:(h2 + 1) * 64, m // 4, (m % 4) * P:(m % 4 + 1) * P],
                                           xdE[0:TS, h * SP_:(h + 1) * SP_], Btm[0:TS, b, (h // R3) * SN:(h // R3 + 1) * SN],
                                           start=True, stop=True)
                    ins.then_inc(sem("ssd_new_local"), 1)
                    e.wait_ge(sem("y_squares"), NJ)
                    e.wait_ge(sem("ssd_new"), 2)
                    parts = [[(0, 0, P), (1, 0, 64)], [(1, 64, P), (2, 0, P)]]
                    for g in range(SG):
                        for h in range(2):
                            for i, (t, a, z) in enumerate(parts[g]):
                                ins = e.matmul(PS[:, 2 * g + h, 0:HALF], ones[a:z, :], halves(xc[a:z, t, :])[:, h, :],
                                               start=(i == 0), stop=(i == 1))
                    ins.then_inc(sem("y_sumsq"), 1)

                @block.scalar
                def _(e):
                    for t in range(CT):
                        w0, cb = convw[:, t:t + 1], cols[:, R_CONVB + t:R_CONVB + t + 1]
                        e.activation(xc[:, t, 0:SEQ], U[:, t, 0:SEQ], ACT.Identity, scale=w0, bias=cb)\
                            .then_inc(sem("conv_first"), 1)
                        e.activation(xc[:, t, SEQ:T].rearrange("p (b i) -> p b i", i=NI), Us[:, t, :, 0:NI],
                                     ACT.Identity, scale=w0, bias=cb).then_inc(sem("conv_first"), 1)
                    for t in range(CT):
                        e.wait_ge(sem("conv_taps"), 6 * (t + 1))
                        e.activation(xc[:, t, :], xc[:, t, :], ACT.Silu).then_inc(sem("conv_silu"), 1)
                    e.wait_ge(sem("dt_abs"), 1)
                    e.activation(dt_abs, dt_abs, ACT.Exp, scale=-1.0).then_inc(sem("dt_exp"), 1)
                    e.wait_ge(sem("dt_one"), 1)
                    e.activation(dt_ln, dt_one, ACT.Ln).then_inc(sem("dt_ln"), 1)
                    e.activation(alog6, alog6, ACT.Exp).then_inc(sem("dt_ln"), 1)
                    for c in range(NTT):
                        _, n = tok(c)
                        e.wait_ge(sem("xt_turned"), c + 1)
                        e.activation(Bt[0:n, c, :], PS[0:n, 2 * (c % 2) + 1, 0:SG * SN], ACT.Copy)\
                            .then_inc(sem("Bt_kept"), 1)
                    for b in range(NB):
                        e.wait_ge(sem("h0_turned"), b + 1)
                        e.activation(h0T[:, b, :], PS[:, 6 + b % 2, 0:SI], ACT.Copy).then_inc(sem("h0T_kept"), 1)
                    for c in range(NTT):
                        _, n = tok(c)
                        e.wait_ge(sem("seg_done"), c + 1)
                        if c >= 1:
                            e.wait_ge(sem("ssd_state"), 2 * c)
                        for i, (a, z) in enumerate(((0, 4), (4, SH))):
                            e.activation(E_[0:n, a:z, 0:n],
                                         PS[0:n, i, 0:(z - a) * n].rearrange("p (h t) -> p h t", t=n), ACT.Exp)
                            ins = e.activation(EC[:, a:z, 0:n],
                                               PS[:, 2 + i, 0:(z - a) * n].rearrange("p (h t) -> p h t", t=n), ACT.Exp)
                        if c == NCH:
                            ins = e.activation(te[0:n, :], PS[0:n, 7, 0:SH], ACT.Exp)
                        ins.then_inc(sem("ssd_exps"), 1)
                    e.wait_ge(sem("decn_done"), 1)
                    e.activation(stT[:], PS[:, 7, 0:SI].rearrange("p (j n) -> p j n", n=P), ACT.Copy)\
                        .then_inc(sem("stT_kept"), 1)
                    e.activation(decN, PS[:, 7, SI:SI + NJ * NB], ACT.Exp).then_inc(sem("decN_ready"), 1)
                    for j in range(NJ):
                        e.wait_ge(sem("y_gated"), j + 1)
                        e.activation(xc[:, j, :], hT[:, j, :], ACT.Square).then_inc(sem("y_squares"), 1)
                    e.wait_ge(sem("y_sumsq"), 1)
                    for g in range(SG):
                        e.activation(halves(xc[:, 3 + g, :]), bank2(2 * g), ACT.Sqrt, scale=float(SG) / SI, bias=epsc[:])\
                            .then_inc(sem("y_root"), 1)

                @block.vector
                def _(e):
                    link = Link(e, "ssd_step")
                    e.wait_ge(sem("ssd_params"), 16 * 3)
                    for h2 in range(2):
                        r = slice(h2 * 64, (h2 + 1) * 64)
                        e.tensor_copy(dcol[r, :], d6[r, h2:SH:2])
                    v = lambda x: x.rearrange("p (c h) -> p c h", h=SH)
                    link(e.tensor_tensor(v(dt_x), dtr[:], bc(bias6, 1, NTT), ALU.add))
                    absolute(e, dt_abs, dt_x).then_inc(sem("dt_abs"), 1)
                    link(e.tensor_scalar(dt_pos, dt_x, 0.0, None, ALU.max))
                    n = 0
                    for t in range(CT):
                        e.wait_ge(sem("conv_first"), 2 * (t + 1))
                        for k in range(1, CONV):
                            w = convw[:, k * CT + t:k * CT + t + 1]
                            xs_ = xc[:, t, SEQ:T].rearrange("p (b i) -> p b i", i=NI)
                            e.scalar_tensor_tensor(out=xc[:, t, 0:SEQ], in0=U[:, t, k:k + SEQ], scalar=w,
                                                   in1=xc[:, t, 0:SEQ], op0=ALU.mult, op1=ALU.add)\
                                .then_inc(sem("conv_taps"), 1)
                            e.scalar_tensor_tensor(out=xs_, in0=Us[:, t, :, k:k + NI], scalar=w, in1=xs_,
                                                   op0=ALU.mult, op1=ALU.add).then_inc(sem("conv_taps"), 1)
                            n += 2
                            if k + 1 < CONV:
                                e.wait_ge(sem("conv_taps"), n)
                    e.wait_ge(sem("dt_exp"), 1)
                    e.tensor_scalar(dt_one, dt_abs, 1.0, None, ALU.add).then_inc(sem("dt_one"), 1)
                    e.wait_ge(sem("dt_one"), 1)
                    link(e.tensor_scalar(dt_eq, dt_one, 1.0, None, ALU.is_equal))
                    e.wait_ge(sem("dt_ln"), 2)
                    link(e.tensor_tensor(dt_ln, dt_ln, dt_eq, ALU.add))
                    link(e.scalar_tensor_tensor(out=dt_one, in0=dt_one, scalar=-1.0, in1=dt_eq, op0=ALU.add, op1=ALU.add))
                    link(e.reciprocal(dt_one, dt_one))
                    link(e.tensor_tensor(dt_ln, dt_ln, dt_abs, ALU.mult))
                    link(e.tensor_tensor(dt_ln, dt_ln, dt_one, ALU.mult))
                    link(e.tensor_tensor(dt_, dt_ln, dt_pos, ALU.add))
                    link(e.scalar_tensor_tensor(out=v(a_), in0=v(dt_), scalar=-1.0, in1=bc(alog6, 1, NTT),
                                                op0=ALU.mult, op1=ALU.mult))
                    e.tensor_copy(aexp[0:TS], bc(a_[0:TS, NCH * SH:NTT * SH], 2, SP_)).then_inc(sem("aexp_ready"), 1)
                    for c in range(NTT):
                        _, n = tok(c)
                        e.wait_ge(sem("xt_turned"), c + 1)
                        e.tensor_copy(xt[0:n, c, :], PS[0:n, 2 * (c % 2), 0:SI]).then_inc(sem("xt_kept"), 1)
                        e.wait_ge(sem("xt_kept"), c + 1)
                        link(e.tensor_tensor(xdt[0:n, c, :].rearrange("p (h q) -> p h q", h=SH),
                                             xt[0:n, c, :].rearrange("p (h q) -> p h q", h=SH),
                                             bc(dt_[0:n, c * SH:(c + 1) * SH], 2, SP_), ALU.mult))
                    e.wait_ge(sem("Bt_kept"), NTT)
                    e.tensor_tensor(Btm[0:TS], bc(Bt[0:TS, NCH, :], 1, NB), bc(bsel[:], 2, SG * SN), ALU.mult)\
                        .then_inc(sem("Btm_ready"), 1)

                    def steps(c):
                        _, n = tok(c)
                        if c >= 2:
                            e.wait_ge(sem("seg_done"), c - 1)
                        e.tensor_tensor(Gm[:, c % 2, :].rearrange("p (h t) -> p h t", t=P)[0:n, :, 0:n],
                                        bc(tri[:] if c < NCH else tri8[:], 1, SH),
                                        bc(a_[0:n, c * SH:(c + 1) * SH], 2, n), ALU.mult).then_inc(sem("gm_ready"), 1)

                    steps(0)
                    e.wait_ge(sem("ssd_zero"), 1)
                    for c in range(NTT):
                        s, n = tok(c)
                        if c + 1 < NTT:
                            steps(c + 1)
                        e.wait_ge(sem("seg_done"), c + 1)
                        if c >= 1:
                            e.wait_ge(sem("y_done"), c)
                        e.tensor_tensor(cbm[0:n, :, 0:n], PS[0:n, 4, 0:SG * n].rearrange("p (g t) -> p g t", t=n),
                                        bc(tri[:] if c < NCH else tri8[:], 1, SG), ALU.mult).then_inc(sem("cbm_ready"), 1)
                        e.wait_ge(sem("cbm_ready"), c + 1)
                        e.wait_ge(sem("ssd_exps"), c + 1)
                        for g in range(SG):
                            hs = slice(g * R3, (g + 1) * R3)
                            e.tensor_tensor(Wt[0:n, hs, 0:n], E_[0:n, hs, 0:n], bc(cbm[0:n, g, 0:n], 1, R3), ALU.mult)
                        e.tensor_tensor(CE[:, 0:R3, 0:n], EC[:, 0:R3, 0:n], bc(xc[:, 5, s], 1, R3), ALU.mult)\
                            .then_inc(sem("ssd_parts"), 1)
                        e.tensor_tensor(CE[:, R3:SH, 0:n], EC[:, R3:SH, 0:n], bc(xc[:, 6, s], 1, R3), ALU.mult)\
                            .then_inc(sem("ssd_parts"), 1)
                        if c >= 1:
                            e.wait_ge(sem("ssd_local"), min(c, NCH))
                        end = E_[0:n, :, P - 1:P].to_broadcast([n, SH, SP_]) if c < NCH else bc(te[0:n, :], 2, SP_)
                        e.tensor_tensor(xdE[0:n, :].rearrange("p (h q) -> p h q", h=SH),
                                        xdt[0:n, c, :].rearrange("p (h q) -> p h q", h=SH), end, ALU.mult)\
                            .then_inc(sem("ssd_parts"), 1)
                        if c < NCH:
                            if c >= 1:
                                e.wait_ge(sem("y_done"), c)
                            new = ST[:, (c + 1) % 2, :].rearrange("p (h q) -> p h q", h=SH)
                            e.tensor_tensor(new, ST[:, c % 2, :].rearrange("p (h q) -> p h q", h=SH),
                                            EC[:, :, P - 1:P].to_broadcast([P, SH, SP_]), ALU.mult)\
                                .then_inc(sem("ssd_state"), 1)
                            e.wait_ge(sem("ssd_state"), 2 * c + 1)
                            e.wait_ge(sem("ssd_local"), c + 1)
                            e.tensor_tensor(ST[:, (c + 1) % 2, :], ST[:, (c + 1) % 2, :], PS[:, 6, 0:SI], ALU.add)\
                                .then_inc(sem("ssd_state"), 1)
                            e.wait_ge(sem("ssd_state"), 2 * c + 2)
                        e.wait_ge(sem("y_done"), c + 1)
                        for j in range(NJ):
                            e.scalar_tensor_tensor(out=hT[:, j, s], in0=xc[:, j, s], scalar=dcol[:, j:j + 1],
                                                   in1=PS[:, 5, j * n:(j + 1) * n], op0=ALU.mult, op1=ALU.add)\
                                .then_inc(sem("y_kept"), 1)
                    e.wait_ge(sem("y_kept"), NJ * NTT)
                    for j in range(NJ):
                        e.tensor_tensor(hT[:, j, :], hT[:, j, :], zT[:, j, :], ALU.mult).then_inc(sem("y_gated"), 1)
                    e.wait_ge(sem("decN_ready"), 1)
                    e.wait_ge(sem("h0_loaded"), 16 * NB)
                    e.tensor_tensor(sN[:], h0n[:], bc(decN.rearrange("p (j b) -> p b j", b=NB), 3, P), ALU.mult)\
                        .then_inc(sem("ssd_new"), 1)
                    e.wait_ge(sem("ssd_new"), 1)
                    e.wait_ge(sem("ssd_new_local"), 1)
                    flat = sN.rearrange("p b j n -> p (b j n)")
                    e.tensor_tensor(flat, PS[:, 0:6, :].rearrange("p b n -> p (b n)"), flat, ALU.add)\
                        .then_inc(sem("ssd_new"), 1)
                    e.wait_ge(sem("y_root"), SG)
                    e.wait_ge(sem("y_squares"), NJ)
                    link(e.reciprocal(xc[:, 3:5, :], xc[:, 3:5, :]))
                    for t, g, a, z in ((0, 0, 0, P), (1, 0, 0, 64), (1, 1, 64, P), (2, 1, 0, P)):
                        e.scalar_tensor_tensor(out=hT[a:z, t, :], in0=hT[a:z, t, :],
                                               scalar=cols[a:z, R_SNORM + t:R_SNORM + t + 1], in1=xc[a:z, 3 + g, :],
                                               op0=ALU.mult, op1=ALU.mult)

            with nc.Block(no_gpsimd_drain=True) as block:
                @block.sync
                def _(e):
                    load_units(e, l, U_OUT + 2, U_FF2 + 2)

                @block.tensor
                def _(e):
                    for d in range(DT):
                        n = U_OUT + d // 2
                        if d % 2 == 0:
                            wait_unit(e, n)
                        if d >= 4:
                            e.wait_ge(sem("mix_added"), d - 3)
                        w = wslot[:, n % 2, 0:DT * 256].rearrange("p (k n) -> p k n", k=DT)
                        for kt in range(DT):
                            for h in range(2):
                                ins = e.matmul(PS[:, 2 * (d % 4) + h, 0:HALF], w[:, kt, (d % 2) * P:(d % 2 + 1) * P],
                                               halves(hT[:, kt, :])[:, h, :], start=(kt == 0), stop=(kt == DT - 1))
                        ins.then_inc(group_done, 1)

                @block.vector
                def _(e):
                    link = Link(e, "mix_gated")
                    for d in range(DT):
                        e.wait_ge(group_done, groups_after(U_OUT - 1) + d + 1)
                        add_to_x(e, link, 5, d, 2 * (d % 4), d % 2).then_inc(sem("mix_added"), 1)

            end_stage()
            ffn_block(l, "f2_", 2, 8, U_FF2, U_FO2, U_END)

            end_stage(w_ready + [group_done])

        (yt,), _ = carve([(NTT, D)])
        with nc.Block() as block:
            q = "out_"

            @block.scalar
            def _(e):
                norm_act(e, q, None)
                for t in range(NTT):
                    n = P if t < NCH else TS
                    e.wait_ge(sem("y_turned"), 2 * t + 2)
                    e.activation(yt[0:n, t, 512:1024], PS[0:n, 2 + 2 * (t % 2) + 1, :], ACT.Copy)\
                        .then_inc(sem("y_kept1"), 1)

            @block.tensor
            def _(e):
                norm_pe(e, q)
                e.wait_ge(sem(q + "h_ready"), DT)
                for t in range(NTT):
                    n = P if t < NCH else TS
                    if t >= 2:
                        e.wait_ge(sem("y_kept0"), t - 1)
                        e.wait_ge(sem("y_kept1"), t - 1)
                    for c in range(2):
                        for d in range(4):
                            ins = e.transpose(PS[0:n, 2 + 2 * (t % 2) + c, d * P:(d + 1) * P],
                                              hT[:, 4 * c + d, t * P:t * P + n], ident[:])
                        ins.then_inc(sem("y_turned"), 1)

            @block.vector
            def _(e):
                norm_dve(e, q, None)
                for t in range(NTT):
                    n = P if t < NCH else TS
                    e.wait_ge(sem("y_turned"), 2 * t + 1)
                    e.tensor_copy(yt[0:n, t, 0:512], PS[0:n, 2 + 2 * (t % 2), :]).then_inc(sem("y_kept0"), 1)

            @block.sync
            def _(e):
                for t in range(NTT):
                    e.wait_ge(sem("y_kept0"), t + 1)
                    e.wait_ge(sem("y_kept1"), t + 1)
                    if t < NCH:
                        e.dma_start(O["y_p"][0, t * P:(t + 1) * P, :], yt[:, t, :]).then_inc(sem("y_stored"), 16)
                    else:
                        e.dma_start(O["y_s"].rearrange("b i d -> (b i) d"), yt[0:TS, t, :])\
                            .then_inc(sem("y_stored"), 16)
                e.wait_ge(sem("y_stored"), 16 * NTT)


_INS = ['x_prompt', 'x_sample', 'c_prompt', 'c_sample', 'state_ssd', 'state_ssd_conv', 'state_gla', 'cache_attn_k',
        'cache_attn_v', 'w_in', 'w_out', 'ssd_conv_w', 'ssd_conv_b', 'ssd_dt_bias', 'ssd_a_log', 'ssd_d',
        'ssd_norm_w', 'gla_w_gate', 'gla_b_gate', 'gla_norm_w', 'norm_w', 'w_mod', 'b_mod', 'ffn1_w_in',
        'ffn1_w_out', 'ffn2_w_in', 'ffn2_w_out', 'norm_f']
_OUTS = [("y_p", (1, SEQ, D)), ("y_s", (NB, NI, D)),
         ("ssd_p", (DEPTH, 1, SH, SP_, SN)), ("ssd_s", (DEPTH, NB, SH, SP_, SN)),
         ("conv_p", (DEPTH, 1, CONV - 1, CT * P)), ("conv_s", (DEPTH, NB, CONV - 1, CT * P)),
         ("gla_p", (DEPTH, 1, GH, GK, GV)), ("gla_s", (DEPTH, NB, GH, GK, GV)),
         ("k_p", (DEPTH, 1, SEQ, AH, AD)), ("k_s", (DEPTH, NB, NI, AH, AD)),
         ("v_p", (DEPTH, 1, SEQ, AH, AD)), ("v_s", (DEPTH, NB, NI, AH, AD))]


def kernel(**inputs):
    import numpy as _np
    import concourse.bacc as _bacc
    from concourse import mybir as _mybir
    from concourse.bass_utils import run_bass_kernel_spmd as _run

    nc = _bacc.Bacc("TRN2", target_bir_lowering=False, num_devices=1)
    arrays, ins, outs = {}, {}, {}
    for name in _INS:
        a = _np.ascontiguousarray(inputs[name])
        arrays[f"in_{name}"] = a
        ins[name] = nc.dram_tensor(f"in_{name}", a.shape, _mybir.dt.from_np(a.dtype), kind="ExternalInput").ap()
    for name, shape in _OUTS:
        outs[name] = nc.dram_tensor(f"out_{name}", shape, _mybir.dt.float32, kind="ExternalOutput").ap()
    program(nc, ins, outs)
    r = _run(nc, [arrays], core_ids=[0])
    return tuple(r.results[0][f"out_{name}"] for name, _ in _OUTS)
```
